# Optimizing a Trainium2 kernel written in Bass

```python
import math
import jax, jax.numpy as jnp
from jax import lax
import numpy as np

D_MODEL = 1024
BATCH = 1
SEQ = 256
DEPTH = 2

HEAD_DIM = 128
N_A_LAYERS = DEPTH // 2
N_B_LAYERS = DEPTH - N_A_LAYERS
MAIN_WIDTH = D_MODEL
POOL_WINDOWS = (2, 4, 8, 16)
POOL_GROUP = MAIN_WIDTH // len(POOL_WINDOWS)
MOBA_HEADS = MAIN_WIDTH // HEAD_DIM
MOBA_BLOCK = 256
MOBA_TOPK = 3
MOBA_CHUNK = 8
MEM_TOKENS = 256
MEM_HEADS = 4
MEM_WIDTH = MEM_HEADS * HEAD_DIM
MIX_WIDTH = MAIN_WIDTH + MEM_WIDTH
ROPE_THETA = 10000.0
PEER_HEADS = 8
PEER_NKEYS = 128
PEER_EXPERTS = PEER_NKEYS * PEER_NKEYS
PEER_TOPK = 16
PEER_QDIM = 256
PEER_HALF = PEER_QDIM // 2
PEER_CHUNK = 128
RMS_EPS = 1e-6
NEG = -1e30

kernel_name = "yoco_pool_moba_peer_hybrid"

def rmsnorm(x, g):
    xf = x.astype(jnp.float32)
    y = xf * lax.rsqrt(jnp.mean(xf * xf, axis=-1, keepdims=True) + RMS_EPS)
    return (y * g.astype(jnp.float32)).astype(x.dtype)

def rope_tables(S):
    inv = 1.0 / (ROPE_THETA ** (jnp.arange(0, HEAD_DIM, 2, dtype=jnp.float32) / HEAD_DIM))
    ang = jnp.arange(S, dtype=jnp.float32)[:, None] * inv[None, :]
    return jnp.cos(ang), jnp.sin(ang)

def apply_rope(x, cos, sin):
    xf = x.astype(jnp.float32)
    x1, x2 = xf[..., : HEAD_DIM // 2], xf[..., HEAD_DIM // 2:]
    return jnp.concatenate([x1 * cos - x2 * sin, x2 * cos + x1 * sin], axis=-1).astype(x.dtype)

def pool_mixer(main, pool_w, pool_scale):
    B, S, _ = main.shape
    t = jnp.arange(S)
    outs = []
    for g, w in enumerate(POOL_WINDOWS):
        xg = main[..., g * POOL_GROUP:(g + 1) * POOL_GROUP].astype(jnp.float32)
        c = lax.cumsum(xg, axis=1)
        lag = jnp.pad(c, ((0, 0), (w, 0), (0, 0)))[:, :S]
        cnt = jnp.minimum(t + 1, w).astype(jnp.float32)[None, :, None]
        d = ((c - lag) / cnt - xg).astype(main.dtype)
        outs.append(jnp.einsum('bsc,ce->bse', d, pool_w[g]))
    return jnp.concatenate(outs, axis=-1) * pool_scale

def memory_attention(qm, mem, w_mem_kv):
    B, S, _ = qm.shape
    M = mem.shape[1]
    kv = mem @ w_mem_kv
    k = kv[..., :MEM_WIDTH].reshape(B, M, MEM_HEADS, HEAD_DIM)
    v = kv[..., MEM_WIDTH:].reshape(B, M, MEM_HEADS, HEAD_DIM)
    q = qm.reshape(B, S, MEM_HEADS, HEAD_DIM)
    logits = jnp.einsum('bshd,bmhd->bhsm', q, k).astype(jnp.float32) * (HEAD_DIM ** -0.5)
    p = jax.nn.softmax(logits, axis=-1).astype(v.dtype)
    return jnp.einsum('bhsm,bmhd->bshd', p, v).reshape(B, S, MEM_WIDTH)

def shared_kv(x, kv_norm_g, w_kv_shared, cos, sin):
    B, S, _ = x.shape
    h = rmsnorm(x, kv_norm_g)
    kv = h @ w_kv_shared
    k = kv[..., :MAIN_WIDTH].reshape(B, S, MOBA_HEADS, HEAD_DIM).transpose(0, 2, 1, 3)
    v = kv[..., MAIN_WIDTH:].reshape(B, S, MOBA_HEADS, HEAD_DIM).transpose(0, 2, 1, 3)
    k = apply_rope(k, cos, sin)
    nb = -(-S // MOBA_BLOCK)
    pad = nb * MOBA_BLOCK - S
    k = jnp.pad(k, ((0, 0), (0, 0), (0, pad), (0, 0))).reshape(B, MOBA_HEADS, nb, MOBA_BLOCK, HEAD_DIM)
    v = jnp.pad(v, ((0, 0), (0, 0), (0, pad), (0, 0))).reshape(B, MOBA_HEADS, nb, MOBA_BLOCK, HEAD_DIM)
    kmean = jnp.mean(k.astype(jnp.float32), axis=3)
    return k, v, kmean

def moba_attention(qmain, k_blocks, v_blocks, kmean, cos, sin):
    B, S, _ = qmain.shape
    H, hd, BLK = MOBA_HEADS, HEAD_DIM, MOBA_BLOCK
    nb = k_blocks.shape[2]
    topk = min(MOBA_TOPK, nb)
    q = apply_rope(qmain.reshape(B, S, H, hd).transpose(0, 2, 1, 3), cos, sin)
    t = jnp.arange(S)
    own = t // BLK
    gate = jnp.einsum('bhsd,bhnd->bhsn', q.astype(jnp.float32), kmean)
    past = jnp.arange(nb)[None, :] < own[:, None]
    gate = jnp.where(past, gate, NEG)
    _, sel = lax.top_k(gate, topk)
    valid = sel < own[:, None]
    nc = S // MOBA_CHUNK

    def to_chunks(a):
        a = a.reshape(a.shape[:2] + (nc, MOBA_CHUNK) + a.shape[3:])
        return jnp.moveaxis(a, 2, 0)

    scale = hd ** -0.5
    bi = jnp.arange(B)[:, None, None, None]
    hi = jnp.arange(H)[None, :, None, None]
    kpos_local = jnp.arange(BLK)

    def attend(args):
        q_c, sel_c, valid_c, pos_c = args
        kg = k_blocks[bi, hi, sel_c]
        vg = v_blocks[bi, hi, sel_c]
        blk = pos_c[0] // BLK
        k_own = lax.dynamic_index_in_dim(k_blocks, blk, axis=2, keepdims=False)
        v_own = lax.dynamic_index_in_dim(v_blocks, blk, axis=2, keepdims=False)
        s_sel = jnp.einsum('bhcd,bhcnkd->bhcnk', q_c, kg).astype(jnp.float32) * scale
        s_sel = jnp.where(valid_c[..., None], s_sel, NEG).reshape(B, H, MOBA_CHUNK, topk * BLK)
        s_own = jnp.einsum('bhcd,bhkd->bhck', q_c, k_own).astype(jnp.float32) * scale
        kpos = blk * BLK + kpos_local
        s_own = jnp.where(kpos[None, :] <= pos_c[:, None], s_own, NEG)
        p = jax.nn.softmax(jnp.concatenate([s_sel, s_own], axis=-1), axis=-1).astype(v_blocks.dtype)
        p_sel = p[..., : topk * BLK].reshape(B, H, MOBA_CHUNK, topk, BLK)
        p_own = p[..., topk * BLK:]
        return (jnp.einsum('bhcnk,bhcnkd->bhcd', p_sel, vg)
                + jnp.einsum('bhck,bhkd->bhcd', p_own, v_own))

    out = lax.map(attend, (to_chunks(q), to_chunks(sel), to_chunks(valid), t.reshape(nc, MOBA_CHUNK)))
    out = jnp.moveaxis(out, 0, 2).reshape(B, H, S, hd)
    return out.transpose(0, 2, 1, 3).reshape(B, S, H * hd)

def peer_ffn(h, wq, subkeys, u, v):
    B, S, D = h.shape
    T = B * S
    ht = h.reshape(T, D)
    q = (ht @ wq).reshape(T, PEER_HEADS, 2, PEER_HALF).astype(jnp.float32)
    s = jnp.einsum('thpd,hpnd->thpn', q, subkeys.astype(jnp.float32))
    sv, si = lax.top_k(s, PEER_TOPK)
    cand = (sv[:, :, 0, :, None] + sv[:, :, 1, None, :]).reshape(T, PEER_HEADS, PEER_TOPK * PEER_TOPK)
    cv, ci = lax.top_k(cand, PEER_TOPK)
    e1 = jnp.take_along_axis(si[:, :, 0], ci // PEER_TOPK, axis=-1)
    e2 = jnp.take_along_axis(si[:, :, 1], ci % PEER_TOPK, axis=-1)
    experts = e1 * PEER_NKEYS + e2
    gates = jax.nn.softmax(cv, axis=-1)
    nc = T // PEER_CHUNK
    E = PEER_HEADS * PEER_TOPK

    def expert_chunk(args):
        xc, ec, gc = args
        a = jnp.einsum('cd,ced->ce', xc, u[ec]).astype(jnp.float32)
        hh = (jax.nn.gelu(a, approximate=False) * gc).astype(v.dtype)
        return jnp.einsum('ce,ced->cd', hh, v[ec])

    out = lax.map(expert_chunk, (ht.reshape(nc, PEER_CHUNK, D),
                                 experts.reshape(nc, PEER_CHUNK, E),
                                 gates.reshape(nc, PEER_CHUNK, E)))
    return out.reshape(B, S, D)

def setup_inputs(seed: int = 0) -> dict:
    key = jax.random.key(seed)
    ks = jax.random.split(key, 20)
    f32 = jnp.float32
    D = D_MODEL

    def nrm(k, shape, scale):
        return jax.random.normal(k, shape, f32) * scale

    return {
        "x": nrm(ks[0], (BATCH, SEQ, D), 1.0),
        "mem": nrm(ks[1], (BATCH, MEM_TOKENS, D), 1.0),
        "norm_mix_g": 1.0 + nrm(ks[2], (DEPTH, D), 0.05),
        "w_in": nrm(ks[3], (DEPTH, D, MIX_WIDTH), D ** -0.5),
        "w_out": nrm(ks[4], (DEPTH, MIX_WIDTH, D), MIX_WIDTH ** -0.5),
        "w_mem_kv": nrm(ks[5], (DEPTH, D, 2 * MEM_WIDTH), D ** -0.5),
        "pool_w": nrm(ks[6], (N_A_LAYERS, len(POOL_WINDOWS), POOL_GROUP, POOL_GROUP), POOL_GROUP ** -0.5),
        "pool_scale": 1.0 + nrm(ks[7], (N_A_LAYERS, MAIN_WIDTH), 0.05),
        "kv_norm_g": 1.0 + nrm(ks[8], (D,), 0.05),
        "w_kv_shared": nrm(ks[9], (D, 2 * MAIN_WIDTH), D ** -0.5),
        "norm_ffn_g": 1.0 + nrm(ks[10], (DEPTH, D), 0.05),
        "peer_wq": nrm(ks[11], (DEPTH, D, PEER_HEADS * PEER_QDIM), D ** -0.5),
        "peer_subkeys": nrm(ks[12], (DEPTH, PEER_HEADS, 2, PEER_NKEYS, PEER_HALF), PEER_HALF ** -0.5),
        "peer_u": nrm(ks[13], (DEPTH, PEER_EXPERTS, D), D ** -0.5),
        "peer_v": nrm(ks[14], (DEPTH, PEER_EXPERTS, D), PEER_HEADS ** -0.5),
        "final_norm_g": 1.0 + nrm(ks[15], (D,), 0.05),
    }

def reference(x, mem, norm_mix_g, w_in, w_out, w_mem_kv, pool_w, pool_scale, kv_norm_g,
              w_kv_shared, norm_ffn_g, peer_wq, peer_subkeys, peer_u, peer_v, final_norm_g):
    S = x.shape[1]
    cos, sin = rope_tables(S)
    shared = None
    for l in range(DEPTH):
        h = rmsnorm(x, norm_mix_g[l])
        proj = h @ w_in[l]
        main, qm = proj[..., :MAIN_WIDTH], proj[..., MAIN_WIDTH:]
        if l < N_A_LAYERS:
            mixed = pool_mixer(main, pool_w[l], pool_scale[l])
        else:
            k_blocks, v_blocks, kmean = shared
            mixed = moba_attention(main, k_blocks, v_blocks, kmean, cos, sin)
        mem_out = memory_attention(qm, mem, w_mem_kv[l])
        x = x + jnp.concatenate([mixed, mem_out], axis=-1) @ w_out[l]
        x = x + peer_ffn(rmsnorm(x, norm_ffn_g[l]), peer_wq[l], peer_subkeys[l], peer_u[l], peer_v[l])
        if l == N_A_LAYERS - 1:
            shared = shared_kv(x, kv_norm_g, w_kv_shared, cos, sin)
    return rmsnorm(x, final_norm_g)


_drawn_inputs = setup_inputs


def setup_inputs(seed=0):
    import zlib

    import numpy as np

    out = dict(_drawn_inputs(seed))
    spreads = {}
    factors = {'kv_norm_g': 3.454}
    for name, (base, spread) in spreads.items():
        noise = np.random.default_rng([zlib.crc32(name.encode()), seed]).standard_normal(out[name].shape)
        drawn = base * np.exp(spread * noise) if base else spread * noise
        out[name] = __import__('jax').numpy.asarray(drawn.astype(out[name].dtype))
    for name, factor in factors.items():
        out[name] = (out[name] * factor).astype(out[name].dtype)
    return out
```

```python
from contextlib import ExitStack

import concourse.bass as bass
from concourse import mybir

F32 = mybir.dt.float32
F32R = mybir.dt.float32r
BF16 = mybir.dt.bfloat16
F16 = mybir.dt.float16
U32 = mybir.dt.uint32
ALU = mybir.AluOpType
ACT = mybir.ActivationFunctionType
AX = mybir.AxisListType.X

P = 128
T = 256
TT = T // P
D = 1024
DC = D // P
HD = 128
MEM_HEADS = 4
MOBA_HEADS = 8
MIXC = DC + MEM_HEADS
WINDOWS = (2, 4, 8, 16)
KEYS = 128
PH = 8
TOPK = 16
PAIRS = PH * 2
HALF = KEYS // 2
TOK = 4
GBLK = T // TOK
GATE_SCALE = 2.0 ** 11
EPS = 1e-6
NEG = -1e30
TAKEN = -3.0e38
SCALE = HD ** -0.5
RING = 4
SPLIT = 4
LEAD = 3
MLEAD = 2
BANKS = 4
BODY = 8
TURNS = HALF // BODY

SLOTS = {"memk": MEM_HEADS, "memv": MEM_HEADS, "in": MIXC, "pool": 2, "out": MIXC, "wq": PAIRS, "keys": 2, "u": KEYS, "v": KEYS, "kv": 16}
LAYER_SLOTS = [["memk", "in", "memv", "pool", "out", "wq", "keys", "u", "v"],
               ["memk", "memv", "kv", "in", "out", "wq", "keys", "u", "v"]]


def plan():
    use, slot, part = {}, {}, {}
    n_use = n_slot = n_part = 0

    def uses(name, n=1):
        nonlocal n_use
        use[name] = n_use
        n_use += n

    def parts(name, n=DC):
        nonlocal n_part
        part[name] = n_part
        n_part += n

    for l, names in enumerate(LAYER_SLOTS):
        for name in names:
            slot[l, name] = n_slot
            n_slot += SLOTS[name]
        if l == 0:
            parts((0, "mem"))
            parts((0, "h_mix"))
            parts((0, "window"))
            uses("norm0")
            uses((l, "memk"), MEM_HEADS)
        uses((l, "in"), MIXC)
        if l == 0:
            uses((l, "memv"), MEM_HEADS)
            uses((l, "memvt"), 2)
        else:
            parts((1, "h_mix"))
        for step, h in attention_order(l):
            uses((l, step, h), DC if step == "pool" else 1)
        uses("norm1" if l == 0 else "norm3")
        parts((l, "h_ffn"))
        uses((l, "wq"), PAIRS)
        uses((l, "score"), PAIRS // 2)
        uses((l, "up0"), HALF - BODY // 2)
        uses((l, "routeT"), 3)
        uses((l, "up0b"), BODY // 2)
        uses((l, "up1"), 2 * HALF)
        uses((l, "down0"), GBLK)
        parts((l, "tile"), KEYS)
        if l == 0:
            uses("norm2")
            parts((1, "mem"))
            uses((1, "memk"), MEM_HEADS)
            uses((1, "memv"), MEM_HEADS)
            uses((1, "memvt"), 2)
            parts("h_kv")
            uses("kv", 16)
            uses("kvt", 4)
    uses("norm4")
    return use, slot, part, n_slot


def attention_heads(l):
    return list(range(MOBA_HEADS if l == 0 else 0, MOBA_HEADS + MEM_HEADS))


def attention_order(l):
    heads = attention_heads(l)
    ahead = 4
    order = [("qk", h) for h in heads[:ahead]]
    if l == 0:
        order.append(("pool", 0))
    for i, h in enumerate(heads):
        order.append(("pt", h))
        if i:
            order.append(("pv", heads[i - 1]))
        if i + ahead < len(heads):
            order.append(("qk", heads[i + ahead]))
    order.append(("pv", heads[-1]))
    return order


def build(nc, stream, x_in, mem_in, gains, small, tables, out):
    use, slot, part, n_slots = plan()
    with ExitStack() as ctx:
        def sb(name, shape, dt=F32):
            return ctx.enter_context(nc.sbuf_tensor(name, shape, dt))

        def sem(name):
            return ctx.enter_context(nc.semaphore(name))

        bank = [ctx.enter_context(nc.psum_tensor(f"bank{i}", [P, 512], F32)) for i in range(BANKS)]
        X = [ctx.enter_context(nc.psum_tensor(f"X{i}", [P, 2, T], F32)) for i in range(DC // 2)]

        def under_a(name, first, n):
            with ExitStack() as under:
                if first:
                    under.enter_context(nc.sbuf_tensor(f"{name}_below", [P, first, T], F32))
                return under.enter_context(nc.sbuf_tensor(name, [P, n, T], F32R))

        mem_hi, mem_lo = under_a("mem_hi", 0, DC), under_a("mem_lo", 12, DC)
        mix_hi, mix_lo = under_a("mix_hi", 52, MIXC), under_a("mix_lo", 24, MIXC)
        qp_hi, qp_lo = under_a("qp_hi", 0, PAIRS), under_a("qp_lo", 16, PAIRS)
        A = sb("A", [P, KEYS, T])
        ring = sb("ring", [P, RING, DC, P])
        w_hi = sb("w_hi", [P, SPLIT, DC, P], F32R)
        w_lo = sb("w_lo", [P, SPLIT, DC, P], F32R)
        m_hi = sb("m_hi", [P, DC, T], F32R)
        m_lo = sb("m_lo", [P, DC, T], F32R)
        rstd = sb("rstd", [P, T])
        var = sb("var", [P, T])
        G = sb("G", [P, 7, DC])
        S = sb("S", [P, 3, P])
        ident, iota, ones = S[:, 0, :], S[:, 1, :], S[:, 2, :]
        e1T = sb("e1T", [P, T], BF16)
        e2T = sb("e2T", [P, T], BF16)
        gT = var
        g2 = sb("g2", [P, T, 2], F16)
        hot1 = sb("hot1", [P, 2, TOK, P], F16)
        hot2 = sb("hot2", [P, TOK, HALF], F16)
        hotg = sb("hotg", [P, 2, TOK, 2, HALF], F16)
        warm = sb("warm", [P, 5])
        nmax = sb("nmax", [P, 12, TT])
        rsum = sb("rsum", [P, 12, TT])
        rinv = sb("rinv", [P, 12, TT])

        def at(a, n):
            return A[:, a:a + n, :]

        memT, memKT, memVT = at(98, 8), at(8, 4), at(112, 4)
        memV = at(20, 4).rearrange("p a b -> p (a b)").rearrange("p (m n) -> p m n", m=2)
        mainT, qmT = at(24, 8), at(32, 4)
        win_a, win_b = at(36, 8), at(44, 8)
        sq = at(44, 8)
        H = at(44, 8)
        x_first = at(24, 8)
        keyT, valT = at(64, 8), at(72, 8)
        val = at(80, 8).rearrange("p a b -> p (a b)").rearrange("p (m n) -> p m n", m=2)
        qT = at(88, 8)
        probs = [at(98 + 2 * h, 2) for h in range(12)]
        cos, sin, mask = A[:, 36, :], A[:, 37, :], at(38, 2)
        swap = at(40, 2)
        inv_count = at(64, 4)
        pT = [at(122, 2), at(124, 2)]

        def flat(a, n):
            return at(a, n).rearrange("p a b -> p (a b)")

        score = flat(64, 16).rearrange("p (t s n) -> p t s n", t=TT, s=PAIRS)
        rest = flat(80, 16).rearrange("p (t s n) -> p t s n", t=TT, s=PAIRS)
        cand = flat(96, 16)
        cand_rest = flat(80, 16)
        hit1, hit2 = flat(64, 16), flat(80, 16)
        sv = flat(112, 2).rearrange("p (t s k) -> p t s k", t=TT, s=PAIRS)
        si = flat(114, 2).bitcast(U32).rearrange("p (t s k) -> p t s k", t=TT, s=PAIRS)
        sif = flat(116, 2)
        cv, ci = flat(118, 1), flat(119, 1).bitcast(U32)
        pos1, pos2 = flat(120, 1).bitcast(U32), flat(121, 1).bitcast(U32)
        pos1f, pos2f = flat(122, 1), flat(123, 1)
        e1, e2 = flat(124, 1), flat(125, 1)
        cexp, gate = flat(126, 1), flat(127, 1)
        csum = var[:, 0:TT * PH]
        cinv = var[:, TT * PH:2 * TT * PH]

        filled = [sem(f"filled{i}") for i in range(RING)]
        slot_used = sem("slot_used")
        bank_full = sem("bank_full")
        bank_read = [sem(f"bank_read{i}") for i in range(BANKS)]
        const_loaded, x_loaded = sem("const_loaded"), sem("x_loaded")
        mem_loaded, table_loaded = sem("mem_loaded"), sem("table_loaded")
        hi_ready = sem("hi_ready")
        slot_begun = sem("slot_begun")
        down_done = sem("down_done")
        out_hi = sem("out_hi")
        mov_hi, mov_lo = sem("mov_hi"), sem("mov_lo")
        x_full = sem("x_full")
        sq_ready, std_ready, h_ready = sem("sq_ready"), sem("std_ready"), sem("h_ready")
        rope_out, window_ready = sem("rope_out"), sem("window_ready")
        max_ready, exp_ready, prob_ready = sem("max_ready"), sem("exp_ready"), sem("prob_ready")
        cdiff_ready, cexp_ready, route_ready = sem("cdiff_ready"), sem("cexp_ready"), sem("route_ready")
        head_lo = sem("head_lo")
        hot_ready = sem("hot_ready")
        dve_step = sem("dve_step")
        stored = sem("stored")
        block = ctx.enter_context(nc.Block())

        @block.sync
        def _(sp):
            sp.dma_start(S[:], small).then_inc(const_loaded, 16)
            sp.dma_start(x_first, x_in).then_inc(x_loaded, 16)
            sp.dma_start(G[:], gains).then_inc(const_loaded, 16)
            for j in range(RING):
                sp.dma_start(ring[:, j], stream[j * P:(j + 1) * P, :]).then_inc(filled[j], 16)
            turns = n_slots // RING
            with sp.Fori(1, turns) as i:
                for j in range(RING):
                    sp.wait_ge(slot_used, i * RING + (j + 1 - RING))
                    sp.dma_start(ring[:, j], stream[bass.ds(i * (RING * P) + j * P, P), :]).then_inc(filled[j], 16)
            for n in range(turns * RING, n_slots):
                sp.wait_ge(slot_used, n + 1 - RING)
                sp.dma_start(ring[:, n % RING], stream[n * P:(n + 1) * P, :]).then_inc(filled[n % RING], 16)
            sp.wait_ge(h_ready, 6 * DC)
            sp.dma_start(out, H[:]).then_inc(stored, 16)
            sp.wait_ge(stored, 16)

        @block.gpsimd
        def _(pool):
            def weight_lo(i, m):
                pool.wait_ge(hi_ready, i + (m + 1))
                nc.gpsimd.tensor_tensor(w_lo[:, m % SPLIT], ring[:, m % RING], w_hi[:, m % SPLIT].bitcast(F32),
                                        ALU.subtract).then_inc(slot_used, 1)

            whole = n_slots // SPLIT * SPLIT
            with pool.Fori(0, whole, SPLIT) as i:
                for m in range(SPLIT):
                    weight_lo(i, m)
            for m in range(whole, n_slots):
                weight_lo(0, m)

        @block.tensor
        def _(pe):
            state = {"use": 0, "tile": 0}

            def open_bank():
                k = state["use"]
                state["use"] += 1
                if k >= BANKS:
                    pe.wait_ge(bank_read[k % BANKS], k // BANKS)
                return bank[k % BANKS]

            def next_slot_tile():
                n, c = divmod(state["tile"], DC)
                state["tile"] += 1
                if c == 0:
                    pe.wait_ge(slot_used, n + 1)
                return n % SPLIT, c, c == 0

            def three_products(o, tile, hi, lo, start, stop, skip=False, begins=False):
                w_h, w_l = w_hi[:, tile[0], tile[1], :], w_lo[:, tile[0], tile[1], :]
                mm = nc.tensor.matmul(o, w_h, hi, start=start, stop=False, skip_group_check=skip)
                if begins:
                    mm.then_inc(slot_begun, 1)
                nc.tensor.matmul(o, w_h, lo, start=False, stop=False, skip_group_check=skip)
                return nc.tensor.matmul(o, w_l, hi, start=False, stop=stop, skip_group_check=skip)

            def project(n_blocks, chunks, moving, first_part):
                for n in range(n_blocks):
                    o = open_bank()
                    for c in range(chunks):
                        b, place, begins = next_slot_tile()
                        hi, lo, p = moving(n, c)
                        if chunks < DC or n == 0:
                            pe.wait_ge(mov_lo, first_part + p + 1)
                        mm = three_products(o[:, 0:T], (b, place), hi, lo, c == 0, c == chunks - 1, begins=begins)
                    mm.then_inc(bank_full, 1)

            def m_chunk(n, c):
                return m_hi[:, c, :], m_lo[:, c, :], c

            def mem_chunk(n, c):
                return mem_hi[:, c, :], mem_lo[:, c, :], c

            def copied(k):
                pe.wait_ge(bank_read[k % BANKS], k // BANKS + 1)

            def norm_sum(k):
                o = open_bank()
                for c in range(DC):
                    if c % 2 == 0:
                        pe.wait_ge(sq_ready, DC // 2 * k + c // 2 + 1)
                    mm = nc.tensor.matmul(o[:, 0:T], ones, sq[:, c, :], start=(c == 0), stop=(c == DC - 1))
                mm.then_inc(bank_full, 1)

            def transposes(pairs):
                o = open_bank()
                for i, src in enumerate(pairs):
                    mm = nc.tensor.transpose(o[:, i * P:(i + 1) * P], src, ident)
                mm.then_inc(bank_full, 1)

            def attention(l):
                heads = attention_heads(l)
                for step, h in attention_order(l):
                    done = (heads.index(h) if h in heads else 0) + 1 + (MEM_HEADS if l == 1 else 0)
                    m = h - MOBA_HEADS
                    if step == "pool":
                        project(DC, 2, lambda n, c: m_chunk(n, n // 2 * 2 + c), part[0, "window"])
                    elif step == "qk":
                        if m >= 0:
                            copied(use[l, "in"] + DC + m)
                            q, k = qmT[:, m, :], memKT[:, m, :]
                        else:
                            pe.wait_ge(rope_out, MOBA_HEADS + h + 1)
                            q, k = qT[:, h, :], keyT[:, h, :]
                        o = open_bank()
                        for t in range(TT):
                            mm = nc.tensor.matmul(o[:, t * T:(t + 1) * T], q[:, t * P:(t + 1) * P], k,
                                                  start=True, stop=True)
                        mm.then_inc(bank_full, 1)
                    elif step == "pt":
                        pe.wait_ge(prob_ready, done)
                        transposes([probs[h][:, t, c * P:(c + 1) * P] for c in range(2) for t in range(TT)])
                    else:
                        copied(use[l, "pt", h])
                        o = open_bank()
                        for c in range(2):
                            v = memV[:, c, m * P:(m + 1) * P] if m >= 0 else val[:, c, h * P:(h + 1) * P]
                            mm = nc.tensor.matmul(o[:, 0:T], v, pT[(done - 1) % 2][:, c, :], start=(c == 0), stop=(c == 1))
                        mm.then_inc(bank_full, 1)

            def gate_block(b, o):
                for t in range(TOK):
                    for p in range(2):
                        mm = nc.tensor.matmul(o[:, t * HALF:(t + 1) * HALF], hot1[:, b, t, :], hotg[:, b, t, p, :],
                                              start=(p == 0), stop=(p == 1))
                mm.then_inc(bank_full, 1)

            def up_tile(l, i, n, k, per):
                pe.wait_ge(slot_used, i * BODY + (slot[l, "u"] + n + 1))
                pe.wait_ge(bank_read[k % BANKS], i * (per // BANKS) + k // BANKS)
                for c in range(DC):
                    last = three_products(bank[k % BANKS][:, 0:T], ((slot[l, "u"] + n) % SPLIT, c), m_hi[:, c, :],
                                          m_lo[:, c, :], c == 0, c == DC - 1, begins=(c == 0))
                last.then_inc(bank_full, 1)

            def up(l):
                with pe.Fori(0, TURNS - 1) as i:
                    for j in range(BODY):
                        up_tile(l, i, j, use[l, "up0"] + j, BODY)
                for j in range(BODY):
                    if j == BODY // 2:
                        pe.wait_ge(route_ready, l + 1)
                        state["use"] = use[l, "routeT"]
                        for a in (e1, e2, gate):
                            transposes([a[:, t * P:(t + 1) * P] for t in range(TT)])
                    e = HALF - BODY + j
                    up_tile(l, 0, e, use[l, "up0"] + e if j < BODY // 2 else use[l, "up0b"] + j - BODY // 2, BODY)
                with pe.Fori(0, TURNS) as i:
                    for j in range(BODY):
                        up_tile(l, i, HALF + j, use[l, "up1"] + 2 * j, 2 * BODY)
                        gate_step(i, use[l, "up1"] + 2 * j + 1, 2 * BODY, 2 * GBLK * l + j)
                state["use"] = use[l, "down0"]
                state["tile"] += KEYS * DC

            def gate_step(i, k, per, g):
                pe.wait_ge(hot_ready, i * BODY + (g + 1))
                pe.wait_ge(bank_read[k % BANKS], i * (per // BANKS) + k // BANKS)
                gate_block(g % 2, bank[k % BANKS])

            def down_half(l, half):
                first_slot = slot[l, "v"] + half * HALF
                first_use = state["use"]
                with pe.Fori(0, TURNS) as i:
                    k = first_use
                    for j in range(BODY):
                        pe.wait_ge(slot_used, i * BODY + (first_slot + j + 1))
                        pe.wait_ge(mov_lo, i * BODY + (part[l, "tile"] + half * HALF + j + 1))
                        for c in range(DC):
                            last = three_products(X[c // 2][:, c % 2, :], ((first_slot + j) % SPLIT, c), m_hi[:, j, :],
                                                  m_lo[:, j, :], False, False, skip=True, begins=(c == 0))
                        last.then_inc(down_done, 1)
                        if half == 0:
                            gate_step(i, k, BODY, GBLK * (2 * l + 1) + j)
                            k += 1
                if half == 0:
                    state["use"] += GBLK
                state["tile"] += HALF * DC

            def values_over_tokens(l):
                copied(use[l, "memv"] + MEM_HEADS - 1)
                for c in range(2):
                    transposes([memVT[:, m, c * P:(c + 1) * P] for m in range(MEM_HEADS)])

            pe.wait_ge(const_loaded, 32)
            for l in range(2):
                if l == 0:
                    pe.wait_ge(x_loaded, 16)
                    for c in range(DC):
                        mm = nc.tensor.matmul(X[c // 2][:, c % 2, :], ident, x_first[:, c, :], start=(c % 2 == 0), stop=False,
                                              skip_group_check=True)
                        if c % 2:
                            mm.then_inc(x_full, 1)
                    norm_sum(0)
                    project(MEM_HEADS, DC, mem_chunk, part[0, "mem"])
                project(MIXC, DC, m_chunk, part[l, "h_mix"])
                if l == 0:
                    project(MEM_HEADS, DC, mem_chunk, part[0, "mem"])
                    values_over_tokens(0)
                copied(use[l, "memvt"] + 1)
                attention(l)
                for n in range(DC):
                    for c in range(MIXC):
                        b, place, begins = next_slot_tile()
                        if n == 0:
                            if l == 0 and c < MOBA_HEADS:
                                copied(use[0, "pool", 0] + c)
                            else:
                                pe.wait_ge(head_lo, c + 1 - MOBA_HEADS if l == 0 else MEM_HEADS + c + 1)
                        mm = three_products(X[n // 2][:, n % 2, :], (b, place), mix_hi[:, c, :], mix_lo[:, c, :],
                                            False, False, skip=True, begins=begins)
                    if n % 2:
                        mm.then_inc(x_full, 1)
                norm_sum(1 if l == 0 else 3)
                project(PAIRS, DC, m_chunk, part[l, "h_ffn"])
                for s2 in range(PAIRS // 2):
                    copied(use[l, "wq"] + 2 * s2 + 1)
                    o = open_bank()
                    for s in (2 * s2, 2 * s2 + 1):
                        b, place, begins = next_slot_tile()
                        w_h, w_l = w_hi[:, b, place, :], w_lo[:, b, place, :]
                        for t in range(TT):
                            a = (s % 2 * TT + t) * P
                            q_h, q_l = qp_hi[:, s, t * P:(t + 1) * P], qp_lo[:, s, t * P:(t + 1) * P]
                            mm = nc.tensor.matmul(o[:, a:a + P], q_h, w_h, start=True, stop=False)
                            if begins and t == 0:
                                mm.then_inc(slot_begun, 1)
                            nc.tensor.matmul(o[:, a:a + P], q_h, w_l, start=False, stop=False)
                            mm = nc.tensor.matmul(o[:, a:a + P], q_l, w_h, start=False, stop=True)
                    mm.then_inc(bank_full, 1)
                up(l)
                down_half(l, 0)
                down_half(l, 1)
                if l == 0:
                    norm_sum(2)
                    project(MEM_HEADS, DC, mem_chunk, part[1, "mem"])
                    project(MEM_HEADS, DC, mem_chunk, part[1, "mem"])
                    values_over_tokens(1)
                    project(16, DC, m_chunk, part["h_kv"])
                    copied(use["kv"] + 15)
                    for c in range(2):
                        for q in range(2):
                            transposes([valT[:, 4 * q + i, c * P:(c + 1) * P] for i in range(4)])
            norm_sum(4)

        @block.scalar
        def _(act):
            def copy_out(k, dst, src, scale=1.0):
                act.wait_ge(bank_full, k + 1)
                ins = nc.scalar.activation(dst, src(bank[k % BANKS]), ACT.Copy, scale=scale)
                ins.then_inc(bank_read[k % BANKS], 1)

            def cols(b):
                return b[:, 0:T]

            def weight_hi(i, n):
                act.wait_ge(filled[n % RING], i * (16 * BODY // RING) + 16 * (n // RING + 1))
                if n >= SPLIT:
                    act.wait_ge(slot_begun, i * BODY + (n - SPLIT + 2))
                nc.scalar.activation(w_hi[:, n % SPLIT], ring[:, n % RING], ACT.Copy).then_inc(hi_ready, 1)

            def tile_hi(i, half, j):
                nc.scalar.activation(m_hi[:, j % BODY, :].rearrange("p (a b) -> p a b", a=1),
                                     A[:, bass.ds(i * BODY + (half * HALF + j), 1), :] if not isinstance(i, int)
                                     else A[:, i * BODY + half * HALF + j:i * BODY + half * HALF + j + 1, :],
                                     ACT.Copy).then_inc(mov_hi, 1)

            hi_done = [0]

            def ahead(n):
                while hi_done[0] <= min(n + LEAD, n_slots - 1):
                    weight_hi(0, hi_done[0])
                    hi_done[0] += 1

            def upper_out(k, dst, scale=1.0):
                act.wait_ge(bank_full, k + 1)
                nc.scalar.activation(dst, cols(bank[k % BANKS]), ACT.Copy, scale=scale).then_inc(out_hi, 1)

            def moving_hi(dst, src, c):
                nc.scalar.activation(dst[:, c, :], src[:, c, :], ACT.Copy).then_inc(mov_hi, 1)

            def h_hi(fill):
                for c in range(DC):
                    act.wait_ge(h_ready, fill * DC + c + 1)
                    moving_hi(m_hi, H, c)

            def square(b, full):
                act.wait_ge(*full)
                nc.scalar.activation(sq[:, 2 * b:2 * b + 2, :], X[b][:], ACT.Square).then_inc(sq_ready, 1)

            def root(k):
                u = use[f"norm{k}"]
                nc.scalar.activation(warm[:, k:k + 1], ones[:, 0:1], ACT.Sqrt)
                act.wait_ge(bank_read[u % BANKS], u // BANKS + 1)
                nc.scalar.activation(rstd[:], var[:], ACT.Sqrt).then_inc(std_ready, 1)

            def rope_copy(k, dst, n):
                act.wait_ge(bank_full, k + 1)
                if n >= 2:
                    act.wait_ge(rope_out, n - 1)
                b = bank[k % BANKS]
                nc.scalar.activation(dst, cols(b), ACT.Copy)
                nc.scalar.activation(swap[0:64, n % 2, :], b[64:128, 0:T], ACT.Copy)
                nc.scalar.activation(swap[64:128, n % 2, :], b[0:64, 0:T], ACT.Copy)\
                  .then_inc(bank_read[k % BANKS], 1)

            def attention(l):
                heads = attention_heads(l)
                base = MEM_HEADS if l == 1 else 0

                def exps(i):
                    h = heads[i]
                    act.wait_ge(max_ready, base + i + 1)
                    for t in range(TT):
                        e = nc.scalar.activation(probs[h][:, t, :], probs[h][:, t, :], ACT.Exp,
                                                 bias=nmax[:, h, t:t + 1], accum_out=rsum[:, h, t:t + 1])
                    e.then_inc(exp_ready, 1)

                def pt(i):
                    k = use[l, "pt", heads[i]]
                    copy_out(k, pT[(base + i) % 2], lambda b: b[:].rearrange("p (c t) -> p c t", c=2))

                if l == 0:
                    for i in range(MEM_HEADS):
                        exps(i)
                    for n in range(DC):
                        ahead(slot[0, "pool"] + n * 2 // DC)
                        upper_out(use[0, "pool", 0] + n, mix_hi[:, n, :], G[:, 6, n:n + 1])
                else:
                    for i in range(3):
                        exps(i)

                def mixed(i):
                    k = use[l, "pv", heads[i]]
                    act.wait_ge(bank_full, k + 1)
                    nc.scalar.activation(mix_hi[:, heads[i], :], cols(bank[k % BANKS]), ACT.Copy)
                    copy_out(k, probs[heads[i]][:, 0, :], cols)

                for i in range(len(heads)):
                    pt(i)
                    if i:
                        mixed(i - 1)
                    if l and i + 3 < len(heads):
                        exps(i + 3)
                mixed(len(heads) - 1)

            def memory_keys(l):
                for n in range(MEM_HEADS):
                    ahead(slot[l, "memk"] + n)
                    copy_out(use[l, "memk"] + n, memKT[:, n, :], cols)

            def memory_values(l):
                for n in range(MEM_HEADS):
                    ahead(slot[l, "memv"] + n)
                    copy_out(use[l, "memv"] + n, memVT[:, n, :], cols)
                for c in range(2):
                    copy_out(use[l, "memvt"] + c, memV[:, c, :], lambda b: b[:])

            for l in range(2):
                if l == 0:
                    act.dma_start(memT, mem_in).then_inc(mem_loaded, 16)
                    act.dma_start(inv_count, tables[:, 4:8, :]).then_inc(table_loaded, 16)
                    act.wait_ge(const_loaded, 32)
                    for b in range(DC // 2):
                        square(b, (x_full, b + 1))
                    act.wait_ge(mem_loaded, 16)
                    for c in range(DC):
                        moving_hi(mem_hi, memT, c)
                    ahead(slot[0, "memk"] - 1)
                    root(0)
                    memory_keys(0)
                    h_hi(0)
                k = use[l, "in"]
                for n in range(DC):
                    ahead(slot[l, "in"] + n)
                    if l == 0:
                        copy_out(k + n, mainT[:, n, :], cols)
                    else:
                        rope_copy(k + n, qT[:, n, :], MOBA_HEADS + n)
                for n in range(MEM_HEADS):
                    ahead(slot[l, "in"] + DC + n)
                    copy_out(k + DC + n, qmT[:, n, :], cols)
                if l == 0:
                    memory_values(0)
                    for c in range(DC):
                        if c % 2 == 0:
                            act.wait_ge(window_ready, c // 2 + 1)
                        moving_hi(m_hi, (win_a, win_b)[c // 2 % 2], c)
                attention(l)
                for i in range(MIXC):
                    ahead(slot[l, "out"] + i)
                    if i % 3 == 2:
                        b = i // 3
                        square(b, (x_full, DC // 2 * (l + 1) + b + 1))
                root(1 if l == 0 else 3)
                h_hi(1 if l == 0 else 4)
                k = use[l, "wq"]
                for n in range(PAIRS):
                    ahead(slot[l, "wq"] + n)
                    upper_out(k + n, qp_hi[:, n, :])
                k = use[l, "score"]
                for s2 in range(PAIRS // 2):
                    ahead(slot[l, "keys"] + s2 // 4)
                    copy_out(k + s2, score[:, :, 2 * s2:2 * s2 + 2, :].rearrange("p t s n -> p s t n"),
                             lambda b: b[:].rearrange("p (s t n) -> p s t n", s=2, t=TT))
                assert hi_done[0] == slot[l, "keys"] + 1 + LEAD + 1
                u, v = slot[l, "u"], slot[l, "v"]
                def gelu(i, e, k, per):
                    weight_hi(i, u + e + LEAD)
                    act.wait_ge(bank_full, i * per + (k + 1))
                    nc.scalar.activation(A[:, bass.ds(i * BODY + e, 1), :],
                                         bank[k % BANKS][:, 0:T].rearrange("p (a b) -> p a b", a=1), ACT.Gelu)\
                      .then_inc(bank_read[k % BANKS], 1)

                with act.Fori(0, TURNS - 1) as i:
                    for j in range(BODY):
                        gelu(i, j, use[l, "up0"] + j, BODY)
                act.wait_ge(cdiff_ready, l + 1)
                nc.scalar.activation(cexp, gate, ACT.Exp).then_inc(cexp_ready, 1)
                for j in range(BODY):
                    if j == BODY // 2:
                        for n, dst in enumerate((e1T, e2T, gT)):
                            copy_out(use[l, "routeT"] + n, dst[:], cols, GATE_SCALE if dst is gT else 1.0)
                    e = HALF - BODY + j
                    gelu(0, e, use[l, "up0"] + e if j < BODY // 2 else use[l, "up0b"] + j - BODY // 2, BODY)
                with act.Fori(0, TURNS) as i:
                    for j in range(BODY):
                        gelu(i, HALF + j, use[l, "up1"] + 2 * j, 2 * BODY)
                for half in range(2):
                    k = use[l, "up1"] + 2 * HALF - 1 if half == 0 else use[l, "down0"] + GBLK - 1
                    act.wait_ge(bank_read[k % BANKS], k // BANKS + 1)
                    for j in range(MLEAD):
                        tile_hi(0, half, j)

                    def turn(i, last):
                        for j in range(BODY):
                            n = v + half * HALF + j + LEAD
                            if n + (i * BODY if last else 0) < n_slots:
                                weight_hi(i, n)
                            if not (last and j + MLEAD >= BODY):
                                tile_hi(i, half, j + MLEAD)

                    with act.Fori(0, TURNS - 1) as i:
                        turn(i, False)
                    turn(TURNS - 1, True)
                hi_done[0] = min(v + KEYS + LEAD, n_slots)
                for b in range(DC // 2):
                    square(b, (down_done, KEYS * (l + 1)))
                if l == 0:
                    act.dma_start(memT, mem_in).then_inc(mem_loaded, 16)
                    act.dma_start(at(36, 4), tables[:, 0:4, :]).then_inc(table_loaded, 16)
                    act.wait_ge(mem_loaded, 32)
                    for c in range(DC):
                        moving_hi(mem_hi, memT, c)
                    root(2)
                    memory_keys(1)
                    memory_values(1)
                    h_hi(2)
                    k = use["kv"]
                    for n in range(MOBA_HEADS):
                        ahead(slot[1, "kv"] + n)
                        rope_copy(k + n, keyT[:, n, :], n)
                    for n in range(MOBA_HEADS):
                        ahead(slot[1, "kv"] + 8 + n)
                        copy_out(k + 8 + n, valT[:, n, :], cols)
                    for c in range(2):
                        for q in range(2):
                            copy_out(use["kvt"] + 2 * c + q, val[:, c, q * 512:(q + 1) * 512], lambda b: b[:])
                    h_hi(3)
            root(4)

        @block.vector
        def _(dve):
            steps = [0]

            def after(ins):
                steps[0] += 1
                ins.then_inc(dve_step, 1)
                dve.wait_ge(dve_step, steps[0])

            def copied(k):
                dve.wait_ge(bank_read[k % BANKS], k // BANKS + 1)

            products = [0]

            def product_lo(k, hi, lo, scale=None):
                products[0] += 1
                dve.wait_ge(out_hi, products[0])
                src = bank[k % BANKS][:, 0:T]
                if scale is None:
                    ins = nc.vector.tensor_tensor(lo, src, hi.bitcast(F32), ALU.subtract)
                else:
                    ins = nc.vector.scalar_tensor_tensor(lo, src, scale, hi.bitcast(F32), ALU.mult, ALU.subtract)
                ins.then_inc(bank_read[k % BANKS], 1)

            def parts_lo(name, src, dst_lo=None, dst_hi=None):
                for c in range(DC):
                    part_lo((dst_lo or m_lo)[:, c, :], src(c), (dst_hi or m_hi)[:, c, :].bitcast(F32), part[name] + c + 1)

            def part_lo(dst, src, hi, n):
                dve.wait_ge(mov_hi, n)
                nc.vector.tensor_tensor(dst, src, hi, ALU.subtract).then_inc(mov_lo, 1)

            def norm_scale(k):
                u = use[f"norm{k}"]
                dve.wait_ge(bank_full, u + 1)
                nc.vector.tensor_scalar(var[:], bank[u % BANKS][:, 0:T], 1.0 / D, EPS, ALU.mult, ALU.add)\
                  .then_inc(bank_read[u % BANKS], 1)
                dve.wait_ge(std_ready, k + 1)
                after(nc.vector.reciprocal(rstd[:], rstd[:]))

            def norm_fill(gain):
                for c in range(DC):
                    nc.vector.scalar_tensor_tensor(H[:, c, :], X[c // 2][:, c % 2, :], G[:, gain, c:c + 1], rstd[:],
                                                   ALU.mult, ALU.mult).then_inc(h_ready, 1)

            def rope(buf, n, k):
                copied(k)
                a, b = buf, swap[:, n % 2, :]
                nc.vector.tensor_tensor(a, a, cos, ALU.mult)
                after(nc.vector.tensor_tensor(b, b, sin, ALU.mult))
                nc.vector.tensor_tensor(a, a, b, ALU.add).then_inc(rope_out, 1)

            def windows():
                copied(use[0, "in"] + MIXC - 1)
                dve.wait_ge(table_loaded, 16)
                src, dst, other = mainT, win_a, win_b
                for g, w in enumerate(WINDOWS):
                    s, a = w // 2, 2 * g
                    nc.vector.tensor_tensor(dst[:, a:DC, s:T], src[:, a:DC, s:T], src[:, a:DC, 0:T - s], ALU.add)
                    after(nc.vector.tensor_copy(dst[:, a:DC, 0:s], src[:, a:DC, 0:s]))
                    src, dst, other = dst, other, dst
                for g in range(4):
                    r = (win_a if g % 2 == 0 else win_b)[:, 2 * g:2 * g + 2, :]
                    after(nc.vector.tensor_tensor(r, r, inv_count[:, g:g + 1, :].broadcast_to([P, 2, T]), ALU.mult))
                    nc.vector.tensor_tensor(r, r, mainT[:, 2 * g:2 * g + 2, :], ALU.subtract).then_inc(window_ready, 1)

            def attention(l):
                heads = attention_heads(l)
                base = MEM_HEADS if l == 1 else 0

                def maxima(i):
                    h = heads[i]
                    k = use[l, "qk", h]
                    dve.wait_ge(bank_full, k + 1)
                    p = probs[h]
                    src = bank[k % BANKS][:].rearrange("p (t k) -> p t k", t=TT)
                    if h < MOBA_HEADS:
                        ins = nc.vector.scalar_tensor_tensor(p, src, SCALE, mask, ALU.mult, ALU.add)
                    else:
                        ins = nc.vector.tensor_scalar(p, src, SCALE, None, ALU.mult)
                    ins.then_inc(bank_read[k % BANKS], 1)
                    copied(k)
                    after(nc.vector.tensor_reduce(rinv[:, h, :], p, AX, ALU.max))
                    nc.vector.tensor_scalar(nmax[:, h, :], rinv[:, h, :], -1.0, None, ALU.mult).then_inc(max_ready, 1)

                def scale(i):
                    h = heads[i]
                    dve.wait_ge(exp_ready, base + i + 1)
                    after(nc.vector.reciprocal(rinv[:, h, :], rsum[:, h, :]))
                    for t in range(TT):
                        ins = nc.vector.tensor_scalar(probs[h][:, t, :], probs[h][:, t, :], rinv[:, h, t:t + 1], None, ALU.mult)
                    ins.then_inc(prob_ready, 1)

                def lower_out(i):
                    h = heads[i]
                    copied(use[l, "pv", h])
                    nc.vector.tensor_tensor(mix_lo[:, h, :], probs[h][:, 0, :], mix_hi[:, h, :].bitcast(F32),
                                            ALU.subtract).then_inc(head_lo, 1)

                if l == 0:
                    for i in range(MEM_HEADS):
                        maxima(i)
                    for i in range(MEM_HEADS):
                        scale(i)
                    for n in range(DC):
                        product_lo(use[0, "pool", 0] + n, mix_hi[:, n, :], mix_lo[:, n, :], G[:, 6, n:n + 1])
                    for i in range(MEM_HEADS):
                        lower_out(i)
                    return
                for i in range(3):
                    maxima(i)
                for i in range(len(heads)):
                    scale(i)
                    if i + 3 < len(heads):
                        maxima(i + 3)
                    if i > 1:
                        lower_out(i - 2)
                lower_out(len(heads) - 2)
                lower_out(len(heads) - 1)

            def top16(values, spare, best, where):
                n = len(values)
                for i in range(n):
                    ins = nc.vector.max(best[i][:, 0:8], values[i])
                after(ins)
                for i in range(n):
                    nc.vector.max_index(where[i][:, 0:8], best[i][:, 0:8], values[i])
                    ins = nc.vector.match_replace(spare[i], best[i][:, 0:8], values[i], TAKEN)
                after(ins)
                for i in range(n):
                    ins = nc.vector.max(best[i][:, 8:16], spare[i])
                after(ins)
                for i in range(n):
                    ins = nc.vector.max_index(where[i][:, 8:16], best[i][:, 8:16], spare[i])
                after(ins)

            def choose(l):
                copied(use[l, "score"] + PAIRS // 2 - 1)
                ts = [(t, s) for t in range(TT) for s in range(PAIRS)]
                top16([score[:, t, s, :] for t, s in ts], [rest[:, t, s, :] for t, s in ts],
                      [sv[:, t, s, :] for t, s in ts], [si[:, t, s, :] for t, s in ts])
                nc.vector.tensor_copy(sif, si.rearrange("p t s k -> p (t s k)"))
                v = sv.rearrange("p t (h s) k -> p (t h) s k", s=2)
                R = TT * PH
                c4 = cand.rearrange("p (r i j) -> p r i j", r=R, i=TOPK)
                shape = [P, R, TOPK, TOPK]
                after(nc.vector.tensor_tensor(c4, v[:, :, 0, :, None].broadcast_to(shape),
                                              v[:, :, 1, None, :].broadcast_to(shape), ALU.add))
                C = TOPK * TOPK
                top16([cand[:, r * C:(r + 1) * C] for r in range(R)], [cand_rest[:, r * C:(r + 1) * C] for r in range(R)],
                      [cv[:, r * TOPK:(r + 1) * TOPK] for r in range(R)], [ci[:, r * TOPK:(r + 1) * TOPK] for r in range(R)])
                c3 = cv.rearrange("p (r k) -> p r k", r=R)
                g3v = gate.rearrange("p (r k) -> p r k", r=R)
                nc.vector.tensor_tensor(g3v, c3, c3[:, :, 0:1].broadcast_to([P, R, TOPK]), ALU.subtract).then_inc(cdiff_ready, 1)
                nc.vector.tensor_scalar(pos1, ci, 4, None, ALU.logical_shift_right)
                after(nc.vector.tensor_scalar(pos2, ci, TOPK - 1, None, ALU.bitwise_and))
                nc.vector.tensor_copy(pos1f, pos1)
                after(nc.vector.tensor_copy(pos2f, pos2))
                sf = sif.rearrange("p (r s k) -> p r s k", r=R, s=2)
                for side, (pos, hit, e) in enumerate(((pos1f, hit1, e1), (pos2f, hit2, e2))):
                    h3 = hit.rearrange("p (a j) -> p a j", j=TOPK)
                    after(nc.vector.tensor_tensor(h3, pos[:, :, None].broadcast_to([P, R * TOPK, TOPK]),
                                                  iota[:, None, 0:TOPK].broadcast_to([P, R * TOPK, TOPK]), ALU.is_equal))
                    h4 = hit.rearrange("p (r k j) -> p r k j", r=R, k=TOPK)
                    after(nc.vector.tensor_tensor(h4, h4, sf[:, :, side, None, :].broadcast_to(shape), ALU.mult))
                    after(nc.vector.tensor_reduce(e, h3, AX, ALU.add))
                dve.wait_ge(cexp_ready, l + 1)
                x3 = cexp.rearrange("p (r k) -> p r k", r=R)
                after(nc.vector.tensor_reduce(csum, x3, AX, ALU.add))
                after(nc.vector.reciprocal(cinv, csum))
                nc.vector.tensor_tensor(g3v, x3, cinv[:, :, None].broadcast_to([P, R, TOPK]), ALU.mult).then_inc(route_ready, 1)

            def split_gates(l):
                copied(use[l, "routeT"] + 2)
                after(nc.vector.tensor_copy(g2[:, :, 0], gT[:]))
                after(nc.vector.tensor_tensor(g2[:, :, 1], gT[:], g2[:, :, 0], ALU.subtract))

            def one(a):
                return a.rearrange("p (a b) -> p a b", a=1)

            def gates_and_tiles(l, gate_half, tile_half):
                half = gate_half
                stride = 2 if half == 0 else 1
                first = use[l, "up1"] + 1 if half == 0 else use[l, "down0"]

                def gate_use(i, b):
                    return i * (stride * BODY) + (first + stride * b)

                def build(i, b, wait=True):
                    if wait:
                        dve.wait_ge(bank_full, gate_use(i, b - 2) + 1)
                    ts = bass.ds(i * (TOK * BODY) + b * TOK, TOK)
                    buf = b % 2
                    if wait or half or l:
                        dve.wait_ge(hot_ready, i * BODY + (GBLK * (2 * l + half) + b))
                    nc.vector.tensor_tensor(hot1[:, buf], iota[:, None, :].broadcast_to([P, TOK, P]),
                                            e1T[:, ts, None].broadcast_to([P, TOK, P]), ALU.is_equal)
                    nc.vector.tensor_tensor(hot2[:], iota[:, None, half * HALF:(half + 1) * HALF].broadcast_to([P, TOK, HALF]),
                                            e2T[:, ts, None].broadcast_to([P, TOK, HALF]), ALU.is_equal).then_inc(dve_step, 1)
                    dve.wait_ge(dve_step, i * BODY + (steps[0] + b + 1))
                    nc.vector.tensor_tensor(hotg[:, buf], hot2[:, :, None, :].broadcast_to([P, TOK, 2, HALF]),
                                            g2[:, ts, :, None].broadcast_to([P, TOK, 2, HALF]), ALU.mult).then_inc(hot_ready, 1)

                def apply(i, b):
                    k4 = (first + stride * b) % BANKS
                    dve.wait_ge(bank_full, gate_use(i, b) + 1)
                    a = A[:, half * HALF:(half + 1) * HALF, bass.ds(i * (TOK * BODY) + b * TOK, TOK)].rearrange("p e t -> p t e")
                    nc.vector.scalar_tensor_tensor(a, bank[k4][:, 0:TOK * HALF].rearrange("p (t e) -> p t e", t=TOK),
                                                   1.0 / GATE_SCALE, a, ALU.mult, ALU.mult)\
                      .then_inc(bank_read[k4], 1)

                def tile_lo(i, j):
                    e = tile_half * HALF + j
                    part_lo(one(m_lo[:, j % BODY, :]), A[:, bass.ds(i * BODY + e, 1), :], one(m_hi[:, j % BODY, :].bitcast(F32)),
                            i * BODY + (part[l, "tile"] + e + 1))

                def turn(i, last):
                    for j in range(BODY):
                        if tile_half is not None and not (last and j + MLEAD >= BODY):
                            tile_lo(i, j + MLEAD)
                        if half is not None:
                            if not (last and j + 1 >= BODY):
                                build(i, j + 1)
                            apply(i, j)

                if tile_half is not None:
                    for j in range(MLEAD):
                        tile_lo(0, j)
                if half is not None:
                    copied(use[l, "up0b"] + BODY // 2 - 1 if half == 0 else use[l, "up1"] + 2 * HALF - 2)
                    build(0, 0, wait=False)
                with dve.Fori(0, TURNS - 1) as i:
                    turn(i, False)
                turn(TURNS - 1, True)
                if half is not None:
                    steps[0] += GBLK

            dve.wait_ge(const_loaded, 32)
            for l in range(2):
                if l == 0:
                    norm_scale(0)
                    parts_lo((0, "mem"), lambda c: memT[:, c, :], mem_lo, mem_hi)
                    norm_fill(0)
                    parts_lo((0, "h_mix"), lambda c: H[:, c, :])
                    windows()
                    parts_lo((0, "window"), lambda c: (win_a, win_b)[c // 2 % 2][:, c, :])
                else:
                    norm_fill(1)
                    parts_lo((1, "h_mix"), lambda c: H[:, c, :])
                    for n in range(MOBA_HEADS):
                        rope(qT[:, n, :], MOBA_HEADS + n, use[l, "in"] + n)
                attention(l)
                norm_scale(1 if l == 0 else 3)
                norm_fill(3 if l == 0 else 4)
                parts_lo((l, "h_ffn"), lambda c: H[:, c, :])
                for n in range(PAIRS):
                    product_lo(use[l, "wq"] + n, qp_hi[:, n, :], qp_lo[:, n, :])
                choose(l)
                split_gates(l)
                gates_and_tiles(l, 0, None)
                gates_and_tiles(l, 1, 0)
                gates_and_tiles(l, None, 1)
                if l == 0:
                    parts_lo((1, "mem"), lambda c: memT[:, c, :], mem_lo, mem_hi)
                    norm_scale(2)
                    norm_fill(2)
                    parts_lo("h_kv", lambda c: H[:, c, :])
                    dve.wait_ge(table_loaded, 32)
                    for n in range(MOBA_HEADS):
                        rope(keyT[:, n, :], n, use["kv"] + n)
            norm_scale(4)
            norm_fill(5)


def kernel(x, mem, norm_mix_g, w_in, w_out, w_mem_kv, pool_w, pool_scale, kv_norm_g, w_kv_shared,
           norm_ffn_g, peer_wq, peer_subkeys, peer_u, peer_v, final_norm_g):
    import numpy as np
    import concourse.bacc as bacc
    from concourse.bass_utils import run_bass_kernel_spmd

    def arr(a):
        return np.asarray(a)

    def blocks(w):
        k, n = w.shape
        return w.reshape(k // P, P, n // P, P).transpose(2, 0, 1, 3).reshape(-1, P, P)

    def pack(tiles):
        return tiles.reshape(-1, DC, P, P).transpose(0, 2, 1, 3).reshape(-1, P, D)

    def columns(v):
        return arr(v).reshape(DC, P).T

    def chunks(a):
        return np.ascontiguousarray(arr(a).reshape(-1, DC, P).transpose(2, 1, 0))

    _, slot, _, n_slots = plan()
    stream = np.empty((n_slots, P, D), np.float32)
    for l, names in enumerate(LAYER_SLOTS):
        for name in names:
            s = slot[l, name]
            place = stream[s:s + SLOTS[name]]
            if name in ("memk", "memv"):
                a = MEM_HEADS * HD * (name == "memv")
                place[:] = pack(blocks(arr(w_mem_kv)[l][:, a:a + MEM_HEADS * HD]))
            elif name == "in":
                place[:] = pack(blocks(arr(w_in)[l]))
            elif name == "pool":
                place[:] = pack(np.concatenate([blocks(w) for w in arr(pool_w)[l]]))
            elif name == "out":
                place[:] = pack(blocks(arr(w_out)[l]))
            elif name == "wq":
                place[:] = pack(blocks(arr(peer_wq)[l]))
            elif name == "keys":
                place[:] = pack(arr(peer_subkeys)[l].reshape(PAIRS, KEYS, P).transpose(0, 2, 1))
            elif name == "kv":
                place[:] = pack(blocks(arr(w_kv_shared)))
            elif name == "u":
                u = arr(peer_u)[l].reshape(KEYS, KEYS, DC, P)
                place[:] = u.transpose(1, 3, 2, 0).reshape(KEYS, P, D)
            else:
                place[:] = arr(peer_v)[l].reshape(KEYS, KEYS, D).transpose(1, 0, 2)
    gains = np.stack([columns(g) for g in (arr(norm_mix_g)[0], arr(norm_mix_g)[1], kv_norm_g, arr(norm_ffn_g)[0],
                                           arr(norm_ffn_g)[1], final_norm_g, arr(pool_scale)[0])], axis=1)
    small = np.stack([np.eye(P), np.tile(np.arange(P), (P, 1)), np.ones((P, P))], axis=1).astype(np.float32)
    t = np.arange(T)
    inv = np.float32(1.0) / (np.float32(10000.0) ** (np.arange(0, HD, 2, dtype=np.float32) / np.float32(HD)))
    angle = (t.astype(np.float32)[:, None] * inv[None, :]).T
    cos, sin = np.cos(angle), np.sin(angle)
    tables = np.zeros((P, 8, T), np.float32)
    tables[:, 0] = np.concatenate([cos, cos])
    tables[:, 1] = np.concatenate([-sin, sin])
    for i in range(TT):
        tables[:, 2 + i] = np.where(t[None, :] <= (i * P + np.arange(P))[:, None], 0.0, NEG)
    for g, w in enumerate(WINDOWS):
        tables[:, 4 + g] = 1.0 / np.minimum(t + 1, w)

    arrays = {"stream": stream.reshape(n_slots * P, D), "x_in": chunks(arr(x)[0]), "mem_in": chunks(arr(mem)[0]),
              "gains": np.ascontiguousarray(gains), "small": small, "tables": tables}
    nc = bacc.Bacc("TRN2", target_bir_lowering=False, num_devices=1)
    args = [nc.dram_tensor(n, a.shape, mybir.dt.from_np(a.dtype), kind="ExternalInput").ap() for n, a in arrays.items()]
    out = nc.dram_tensor("out", (P, DC, T), F32, kind="ExternalOutput").ap()
    build(nc, *args, out)
    r = run_bass_kernel_spmd(nc, [arrays], core_ids=[0])
    return r.results[0]["out"].transpose(2, 1, 0).reshape(1, T, D)
```

```python
from contextlib import ExitStack

import concourse.bass as bass
from concourse import mybir

F32 = mybir.dt.float32
F32R = mybir.dt.float32r
BF16 = mybir.dt.bfloat16
F16 = mybir.dt.float16
U32 = mybir.dt.uint32
ALU = mybir.AluOpType
ACT = mybir.ActivationFunctionType
AX = mybir.AxisListType.X

P = 128
T = 256
TT = T // P
D = 1024
DC = D // P
HD = 128
MEM_HEADS = 4
MOBA_HEADS = 8
MIXC = DC + MEM_HEADS
WINDOWS = (2, 4, 8, 16)
KEYS = 128
PH = 8
TOPK = 16
PAIRS = PH * 2
HALF = KEYS // 2
TOK = 4
GBLK = T // TOK
GATE_SCALE = 2.0 ** 11
EPS = 1e-6
NEG = -1e30
TAKEN = -3.0e38
SCALE = HD ** -0.5
RING = 4
SPLIT = 4
AHEAD = 4
LEAD = 3
MLEAD = 2
BANKS = 4
BODY = 8
TURNS = HALF // BODY
LATE = HALF + BODY // 2
GATE_BANK, TABLE_BANK = 2, 3

SLOTS = {"memk": MEM_HEADS, "memv": MEM_HEADS, "in": MIXC, "pool": 2, "out": MIXC, "wq": PAIRS, "keys": 2, "u": KEYS, "v": KEYS, "kv": 16}
LAYER_SLOTS = [["memk", "in", "memv", "pool", "out", "wq", "keys", "u", "v"],
               ["memk", "memv", "kv", "in", "out", "wq", "keys", "u", "v"]]


def plan():
    use, slot, part = {}, {}, {}
    n_use = n_slot = n_part = 0

    def uses(name, n=1):
        nonlocal n_use
        use[name] = n_use
        n_use += n

    def parts(name, n=DC):
        nonlocal n_part
        part[name] = n_part
        n_part += n

    for l, names in enumerate(LAYER_SLOTS):
        for name in names:
            slot[l, name] = n_slot
            n_slot += SLOTS[name]
        if l == 0:
            parts((0, "mem"))
            parts((0, "h_mix"))
            parts((0, "window"))
            uses((l, "memk"), MEM_HEADS // 2)
            uses("norm0")
            uses((l, "memk2"), MEM_HEADS // 2)
        uses((l, "in"), MIXC if l == 0 else DC)
        for i in range(AHEAD):
            if l:
                uses((1, "qm", i))
            else:
                use[0, "qm", i] = use[0, "in"] + DC + i
            uses((l, "qk", attention_heads(l)[i]))
        if l == 0:
            uses((l, "memv"), MEM_HEADS)
            uses((l, "memvt"), 2)
        else:
            parts((1, "h_mix"))
        for step, h in attention_order(l):
            uses((l, step, h), DC if step == "pool" else 1)
        uses("norm1" if l == 0 else "norm3")
        parts((l, "h_ffn"))
        uses((l, "wq"), PAIRS)
        uses((l, "score"), PAIRS)
        uses((l, "up0"), HALF - BODY // 2)
        uses((l, "routeT"), 3)
        parts((l, "tile"), KEYS)
        if l == 0:
            parts((1, "mem"))
            uses((1, "memk"), 1)
            uses("norm2")
            uses((1, "memk2"), MEM_HEADS - 1)
            uses((1, "memv"), MEM_HEADS)
            parts("h_kv")
            uses("kv", 16)
            uses((1, "memvt"), 2)
            uses("kvt", 4)
    uses("norm4")
    return use, slot, part, n_slot


def last_use(b, k):
    return k - (k - b) % BANKS


def attention_heads(l):
    return list(range(MOBA_HEADS if l == 0 else 0, MOBA_HEADS + MEM_HEADS))


def attention_order(l):
    heads = attention_heads(l)
    order = [] if l else [("pool", 0)]
    for i, h in enumerate(heads):
        order.append(("pt", h))
        if i:
            order.append(("pv", heads[i - 1]))
        if i + AHEAD < len(heads):
            order.append(("qk", heads[i + AHEAD]))
    order.append(("pv", heads[-1]))
    return order


def build(nc, stream, x_in, mem_in, gains, small, tables, out):
    use, slot, part, n_slots = plan()
    with ExitStack() as ctx:
        def sb(name, shape, dt=F32):
            return ctx.enter_context(nc.sbuf_tensor(name, shape, dt))

        def sem(name):
            return ctx.enter_context(nc.semaphore(name))

        bank = [ctx.enter_context(nc.psum_tensor(f"bank{i}", [P, 512], F32)) for i in range(BANKS)]
        X = [ctx.enter_context(nc.psum_tensor(f"X{i}", [P, 2, T], F32)) for i in range(DC // 2)]

        def under_a(name, first, n):
            with ExitStack() as under:
                if first:
                    under.enter_context(nc.sbuf_tensor(f"{name}_below", [P, first, T], F32))
                return under.enter_context(nc.sbuf_tensor(name, [P, n, T], F32R))

        mem_hi, mem_lo = under_a("mem_hi", 0, DC), under_a("mem_lo", 12, DC)
        mix_hi, mix_lo = under_a("mix_hi", 52, MIXC), under_a("mix_lo", 24, MIXC)
        qp_hi, qp_lo = under_a("qp_hi", 0, PAIRS), under_a("qp_lo", 16, PAIRS)
        A = sb("A", [P, KEYS, T])
        ring = sb("ring", [P, RING, DC, P])
        w_parts = sb("w_parts", [P, SPLIT, 2, DC, P], F32R)
        w_hi, w_lo = w_parts[:, :, 0], w_parts[:, :, 1]
        m_hi = sb("m_hi", [P, DC, T], F32R)
        m_lo = sb("m_lo", [P, DC, T], F32R)
        rstd = sb("rstd", [P, T])
        var = sb("var", [P, T])
        G = sb("G", [P, 7, DC])
        S = sb("S", [P, 3, P])
        ident, iota, ones = S[:, 0, :], S[:, 1, :], S[:, 2, :]
        e1T = sb("e1T", [P, T], BF16)
        e2T = sb("e2T", [P, T], BF16)
        gT = var
        g2 = sb("g2", [P, T, 2], F16)
        hot1 = sb("hot1", [P, 2, TOK, P], F16)
        hot2 = sb("hot2", [P, TOK, HALF], F16)
        hotg = sb("hotg", [P, 2, TOK, 2, HALF], F16)
        warm = sb("warm", [P, 5])
        eps = sb("eps", [P, 1])
        iota_bank = bank[TABLE_BANK][:, 0:P]
        g_first = bank[TABLE_BANK][:, P:P + T]
        nmax = sb("nmax", [P, 12, TT])
        rsum = sb("rsum", [P, 12, TT])
        rinv = sb("rinv", [P, 12, TT])

        def at(a, n):
            return A[:, a:a + n, :]

        memT, memKT, memVT = at(98, 8), at(8, 4), at(98, 4)
        memV = at(20, 4).rearrange("p a b -> p (a b)").rearrange("p (m n) -> p m n", m=2)
        mainT, qmT = at(24, 8), at(32, 4)
        win_a, win_b = at(36, 8), at(44, 8)
        sq = at(44, 8)
        H = at(44, 8)
        x_first = at(24, 8)
        keyT, valT = at(64, 8), at(72, 8)
        val = at(80, 8).rearrange("p a b -> p (a b)").rearrange("p (m n) -> p m n", m=2)
        qT = at(88, 8)
        probs = [at(98 + 2 * h, 2) for h in range(12)]
        cos, sin, mask = A[:, 36, :], A[:, 37, :], at(38, 2)
        swap = at(40, 2)
        inv_count = at(64, 4)
        pT = [at(122, 2), at(124, 2)]

        def flat(a, n):
            return at(a, n).rearrange("p a b -> p (a b)")

        score = flat(64, 16).rearrange("p (t s n) -> p t s n", t=TT, s=PAIRS)
        rest = flat(80, 16).rearrange("p (t s n) -> p t s n", t=TT, s=PAIRS)
        cand = flat(96, 16)
        cand_rest = flat(80, 16)
        hit1, hit2 = flat(64, 16), flat(80, 16)
        sv = flat(112, 2).rearrange("p (t s k) -> p t s k", t=TT, s=PAIRS)
        si = flat(114, 2).bitcast(U32).rearrange("p (t s k) -> p t s k", t=TT, s=PAIRS)
        sif = flat(116, 2)
        cv, ci = flat(118, 1), flat(119, 1).bitcast(U32)
        pos1, pos2 = flat(120, 1).bitcast(U32), flat(121, 1).bitcast(U32)
        pos1f, pos2f = flat(122, 1), flat(123, 1)
        e1, e2 = flat(124, 1), flat(125, 1)
        cexp, gate = flat(126, 1), flat(127, 1)
        csum = var[:, 0:TT * PH]
        cinv = var[:, TT * PH:2 * TT * PH]

        def scores_of(b):
            return b[:].rearrange("p (t a n) -> p t a n", t=TT, a=2)

        filled = [sem(f"filled{i}") for i in range(RING)]
        slot_used = sem("slot_used")
        bank_full = sem("bank_full")
        bank_read = [sem(f"bank_read{i}") for i in range(BANKS)]
        act_full, act_read = sem("act_full"), sem("act_read")
        gate_full, gate_read = sem("gate_full"), sem("gate_read")
        const_loaded, x_loaded = sem("const_loaded"), sem("x_loaded")
        gains_loaded, eps_ready = sem("gains_loaded"), sem("eps_ready")
        mem_loaded, table_loaded = sem("mem_loaded"), sem("table_loaded")
        hi_ready = sem("hi_ready")
        slot_begun = sem("slot_begun")
        down_done = sem("down_done")
        out_hi = sem("out_hi")
        mov_hi, mov_lo = sem("mov_hi"), sem("mov_lo")
        x_full = sem("x_full")
        sq_ready, h_ready = sem("sq_ready"), sem("h_ready")
        rope_out, window_ready = sem("rope_out"), sem("window_ready")
        max_ready, exp_ready, prob_ready = sem("max_ready"), sem("exp_ready"), sem("prob_ready")
        cdiff_ready, cexp_ready, route_ready = sem("cdiff_ready"), sem("cexp_ready"), sem("route_ready")
        head_lo = sem("head_lo")
        score_part = sem("score_part")
        hot_ready = sem("hot_ready")
        dve_step = sem("dve_step")
        stored = sem("stored")
        block = ctx.enter_context(nc.Block())

        @block.sync
        def _(sp):
            for j in range(RING):
                sp.dma_start(ring[:, j], stream[j * P:(j + 1) * P, :]).then_inc(filled[j], 16)
                if j == 0:
                    sp.dma_start(S[:], small).then_inc(const_loaded, 16)
                    sp.dma_start(x_first, x_in).then_inc(x_loaded, 16)
                    sp.dma_start(G[:], gains).then_inc(gains_loaded, 16)
            turns = n_slots // RING
            with sp.Fori(1, turns) as i:
                for j in range(RING):
                    sp.wait_ge(slot_used, i * RING + (j + 1 - RING))
                    sp.dma_start(ring[:, j], stream[bass.ds(i * (RING * P) + j * P, P), :]).then_inc(filled[j], 16)
            for n in range(turns * RING, n_slots):
                sp.wait_ge(slot_used, n + 1 - RING)
                sp.dma_start(ring[:, n % RING], stream[n * P:(n + 1) * P, :]).then_inc(filled[n % RING], 16)
            for c in range(0, DC, 2):
                sp.wait_ge(h_ready, 5 * DC + c + 2)
                sp.dma_start(out[:, c:c + 2, :], H[:, c:c + 2, :]).then_inc(stored, 16)
            sp.wait_ge(stored, DC // 2 * 16)

        @block.gpsimd
        def _(pool):
            def weight_lo(i, m):
                pool.wait_ge(hi_ready, i + (m + 1))
                nc.gpsimd.tensor_tensor(w_lo[:, m % SPLIT], ring[:, m % RING], w_hi[:, m % SPLIT].bitcast(F32),
                                        ALU.subtract).then_inc(slot_used, 1)

            whole = n_slots // SPLIT * SPLIT
            with pool.Fori(0, whole, SPLIT) as i:
                for m in range(SPLIT):
                    weight_lo(i, m)
            for m in range(whole, n_slots):
                weight_lo(0, m)

        @block.tensor
        def _(pe):
            state = {"use": 0, "tile": 0}

            def open_bank():
                k = state["use"]
                state["use"] += 1
                if k >= BANKS:
                    pe.wait_ge(bank_read[k % BANKS], k // BANKS)
                return bank[k % BANKS]

            def next_slot_tile():
                n, c = divmod(state["tile"], DC)
                state["tile"] += 1
                if c == 0:
                    pe.wait_ge(slot_used, n + 1)
                return n % SPLIT, c, c == 0

            def three_products(o, tile, hi, lo, start, stop, skip=False, begins=False):
                w_h, w_l = w_hi[:, tile[0], tile[1], :], w_lo[:, tile[0], tile[1], :]
                mm = nc.tensor.matmul(o, w_h, hi, start=start, stop=False, skip_group_check=skip)
                if begins:
                    mm.then_inc(slot_begun, 1)
                nc.tensor.matmul(o, w_h, lo, start=False, stop=False, skip_group_check=skip)
                return nc.tensor.matmul(o, w_l, hi, start=False, stop=stop, skip_group_check=skip)

            def project(n_blocks, chunks, moving, first_part):
                for n in range(n_blocks):
                    o = open_bank()
                    for c in range(chunks):
                        b, place, begins = next_slot_tile()
                        hi, lo, p = moving(n, c)
                        if chunks < DC or n == 0:
                            pe.wait_ge(mov_lo, first_part + p + 1)
                        mm = three_products(o[:, 0:T], (b, place), hi, lo, c == 0, c == chunks - 1, begins=begins)
                    mm.then_inc(bank_full, 1)

            def project_pair(first_part):
                o, n = (open_bank(), open_bank()), state["tile"] // DC
                pe.wait_ge(slot_used, n + 2)
                for c in range(DC):
                    pe.wait_ge(mov_lo, first_part + c + 1)
                    for q in range(2):
                        mm = three_products(o[q][:, 0:T], ((n + q) % SPLIT, c), m_hi[:, c, :], m_lo[:, c, :], c == 0, c == DC - 1,
                                            begins=(c == (0, DC - 1)[q]))
                        if c == DC - 1:
                            mm.then_inc(bank_full, 1)
                state["tile"] += 2 * DC

            def m_chunk(n, c):
                return m_hi[:, c, :], m_lo[:, c, :], c

            def mem_chunk(n, c):
                return mem_hi[:, c, :], mem_lo[:, c, :], c

            def copied(k):
                pe.wait_ge(bank_read[k % BANKS], k // BANKS + 1)

            def norm_sum(k):
                o = open_bank()
                for c in range(DC):
                    if c % 2 == 0:
                        pe.wait_ge(sq_ready, DC // 2 * k + c // 2 + 1)
                    mm = nc.tensor.matmul(o[:, 0:T], ones, sq[:, c, :], start=(c == 0), stop=(c == DC - 1))
                mm.then_inc(bank_full, 1)

            def transposes(pairs):
                o = open_bank()
                for i, src in enumerate(pairs):
                    mm = nc.tensor.transpose(o[:, i * P:(i + 1) * P], src, ident)
                mm.then_inc(bank_full, 1)

            def attention(l, order):
                heads = attention_heads(l)
                for step, h in order:
                    done = (heads.index(h) if h in heads else 0) + 1 + (MEM_HEADS if l == 1 else 0)
                    m = h - MOBA_HEADS
                    if step == "pool":
                        project(DC, 2, lambda n, c: m_chunk(n, n // 2 * 2 + c), part[0, "window"])
                    elif step == "qk":
                        if m >= 0:
                            copied(use[l, "qm", m])
                            q, k = qmT[:, m, :], memKT[:, m, :]
                        else:
                            pe.wait_ge(rope_out, MOBA_HEADS + h + 1)
                            q, k = qT[:, h, :], keyT[:, h, :]
                        o = open_bank()
                        for t in range(TT):
                            mm = nc.tensor.matmul(o[:, t * T:(t + 1) * T], q[:, t * P:(t + 1) * P], k,
                                                  start=True, stop=True)
                        mm.then_inc(bank_full, 1)
                    elif step == "pt":
                        pe.wait_ge(prob_ready, done)
                        transposes([probs[h][:, t, c * P:(c + 1) * P] for c in range(2) for t in range(TT)])
                    else:
                        copied(use[l, "pt", h])
                        o = open_bank()
                        for c in range(2):
                            v = memV[:, c, m * P:(m + 1) * P] if m >= 0 else val[:, c, h * P:(h + 1) * P]
                            mm = nc.tensor.matmul(o[:, 0:T], v, pT[(done - 1) % 2][:, c, :], start=(c == 0), stop=(c == 1))
                        mm.then_inc(bank_full, 1)

            def gate_block(b, o):
                for t in range(TOK):
                    for p in range(2):
                        mm = nc.tensor.matmul(o[:, t * HALF:(t + 1) * HALF], hot1[:, b, t, :], hotg[:, b, t, p, :],
                                              start=(p == 0), stop=(p == 1))
                mm.then_inc(gate_full, 1)

            def up_tile(l, i, n, o):
                pe.wait_ge(slot_used, i * BODY + (slot[l, "u"] + n + 1))
                for c in range(DC):
                    last = three_products(o[:, 0:T], ((slot[l, "u"] + n) % SPLIT, c), m_hi[:, c, :],
                                          m_lo[:, c, :], c == 0, c == DC - 1, begins=(c == 0))
                return last

            def early_tile(l, i, n):
                k = use[l, "up0"] + n
                pe.wait_ge(bank_read[k % BANKS], i * (BODY // BANKS) + k // BANKS)
                up_tile(l, i, n, bank[k % BANKS]).then_inc(bank_full, 1)

            def late_tile(l, i, a):
                if a >= 2:
                    pe.wait_ge(act_read, i * BODY + (LATE * l + a - 1))
                else:
                    copied(last_use(a, use[l, "routeT"] + 2))
                up_tile(l, i, KEYS - LATE + a, bank[a % 2]).then_inc(act_full, 1)

            def up(l):
                with pe.Fori(0, TURNS - 1) as i:
                    for j in range(BODY):
                        early_tile(l, i, j)
                for j in range(BODY // 2):
                    early_tile(l, 0, HALF - BODY + j)
                pe.wait_ge(route_ready, l + 1)
                state["use"] = use[l, "routeT"]
                for a in (e1, e2, gate):
                    transposes([a[:, t * P:(t + 1) * P] for t in range(TT)])
                for a in range(BODY // 2):
                    late_tile(l, 0, a)
                with pe.Fori(0, TURNS) as i:
                    for j in range(BODY):
                        late_tile(l, i, BODY // 2 + j)
                        gate_step(l, i, 2 * GBLK * l + j)
                state["tile"] += KEYS * DC

            def gate_step(l, i, g):
                pe.wait_ge(hot_ready, i * BODY + (g + 1))
                pe.wait_ge(gate_read, i * BODY + (g + l + 1))
                gate_block(g % 2, bank[GATE_BANK])

            def down_half(l, half):
                first_slot = slot[l, "v"] + half * HALF
                with pe.Fori(0, TURNS) as i:
                    for j in range(BODY):
                        pe.wait_ge(slot_used, i * BODY + (first_slot + j + 1))
                        pe.wait_ge(mov_lo, i * BODY + (part[l, "tile"] + half * HALF + j + 1))
                        for c in range(DC):
                            last = three_products(X[c // 2][:, c % 2, :], ((first_slot + j) % SPLIT, c), m_hi[:, j, :],
                                                  m_lo[:, j, :], False, False, skip=True, begins=(c == 0))
                            if c == 1 and half == 0:
                                gate_step(l, i, GBLK * (2 * l + 1) + j)
                        last.then_inc(down_done, 1)
                state["tile"] += HALF * DC

            def values_over_tokens(l):
                copied(use[l, "memv"] + MEM_HEADS - 1)
                for c in range(2):
                    transposes([memVT[:, m, c * P:(c + 1) * P] for m in range(MEM_HEADS)])

            for l in range(2):
                if l == 0:
                    project(1, DC, mem_chunk, part[0, "mem"])
                    pe.wait_ge(const_loaded, 16)
                    pe.wait_ge(x_loaded, 16)
                    for c in range(DC):
                        mm = nc.tensor.matmul(X[c // 2][:, c % 2, :], ident, x_first[:, c, :], start=(c % 2 == 0), stop=False,
                                              skip_group_check=True)
                        if c % 2:
                            mm.then_inc(x_full, 1)
                    project(1, DC, mem_chunk, part[0, "mem"])
                    norm_sum(0)
                    project(2, DC, mem_chunk, part[0, "mem"])
                project_pair(part[l, "h_mix"])
                if l == 0:
                    project(MIXC - 2, DC, m_chunk, part[l, "h_mix"])
                    attention(0, [("qk", h) for h in attention_heads(0)])
                else:
                    project(DC - 2, DC, m_chunk, part[l, "h_mix"])
                    for i in range(MEM_HEADS):
                        project(1, DC, m_chunk, part[l, "h_mix"])
                        attention(1, [("qk", i)])
                if l == 0:
                    project(MEM_HEADS, DC, mem_chunk, part[0, "mem"])
                    values_over_tokens(0)
                copied(use[l, "memvt"] + 1)
                attention(l, attention_order(l))
                for n in range(DC):
                    for c in range(MIXC):
                        b, place, begins = next_slot_tile()
                        if n == 0:
                            if l == 0 and c < MOBA_HEADS:
                                copied(use[0, "pool", 0] + c)
                            else:
                                pe.wait_ge(head_lo, c + 1 - MOBA_HEADS if l == 0 else MEM_HEADS + c + 1)
                        mm = three_products(X[n // 2][:, n % 2, :], (b, place), mix_hi[:, c, :], mix_lo[:, c, :],
                                            False, False, skip=True, begins=begins)
                    if n % 2:
                        mm.then_inc(x_full, 1)
                norm_sum(1 if l == 0 else 3)
                project_pair(part[l, "h_ffn"])
                project(PAIRS - 2, DC, m_chunk, part[l, "h_ffn"])
                for n in range(PAIRS):
                    copied(use[l, "wq"] + n)
                    o = open_bank()
                    b, place, begins = next_slot_tile()
                    for t in range(TT):
                        both = o[:, t * 2 * P:(t + 1) * 2 * P].rearrange("p (a n) -> p a n", a=2)
                        mm = nc.tensor.matmul(both, qp_hi[:, n, t * P:(t + 1) * P], w_parts[:, b, :, place, :],
                                              start=True, stop=False, skip_group_check=True)
                        if begins and t == 0:
                            mm.then_inc(slot_begun, 1)
                        mm = nc.tensor.matmul(both[:, 0, :], qp_lo[:, n, t * P:(t + 1) * P], w_hi[:, b, place, :],
                                              start=False, stop=True, skip_group_check=True)
                    mm.then_inc(bank_full, 1)
                up(l)
                down_half(l, 0)
                down_half(l, 1)
                if l == 0:
                    project(1, DC, mem_chunk, part[1, "mem"])
                    norm_sum(2)
                    project(MEM_HEADS - 1, DC, mem_chunk, part[1, "mem"])
                    project(MEM_HEADS, DC, mem_chunk, part[1, "mem"])
                    project(16, DC, m_chunk, part["h_kv"])
                    values_over_tokens(1)
                    copied(use["kv"] + 15)
                    for c in range(2):
                        for q in range(2):
                            transposes([valT[:, 4 * q + i, c * P:(c + 1) * P] for i in range(4)])
            norm_sum(4)

        @block.scalar
        def _(act):
            def copy_out(k, dst, src, scale=1.0):
                act.wait_ge(bank_full, k + 1)
                ins = nc.scalar.activation(dst, src(bank[k % BANKS]), ACT.Copy, scale=scale)
                ins.then_inc(bank_read[k % BANKS], 1)

            def cols(b):
                return b[:, 0:T]

            def weight_hi(i, n):
                act.wait_ge(filled[n % RING], i * (16 * BODY // RING) + 16 * (n // RING + 1))
                if n >= SPLIT:
                    act.wait_ge(slot_begun, i * BODY + (n - SPLIT + 2))
                nc.scalar.activation(w_hi[:, n % SPLIT], ring[:, n % RING], ACT.Copy).then_inc(hi_ready, 1)

            def tile_hi(i, half, j):
                nc.scalar.activation(m_hi[:, j % BODY, :].rearrange("p (a b) -> p a b", a=1),
                                     A[:, bass.ds(i * BODY + (half * HALF + j), 1), :] if not isinstance(i, int)
                                     else A[:, i * BODY + half * HALF + j:i * BODY + half * HALF + j + 1, :],
                                     ACT.Copy).then_inc(mov_hi, 1)

            hi_done = [0]

            def ahead(n):
                while hi_done[0] <= min(n + LEAD, n_slots - 1):
                    weight_hi(0, hi_done[0])
                    hi_done[0] += 1

            def upper_out(k, dst, scale=1.0):
                act.wait_ge(bank_full, k + 1)
                nc.scalar.activation(dst, cols(bank[k % BANKS]), ACT.Copy, scale=scale).then_inc(out_hi, 1)

            def moving_hi(dst, src, c):
                nc.scalar.activation(dst[:, c, :], src[:, c, :], ACT.Copy).then_inc(mov_hi, 1)

            def h_hi(fill, n):
                for c in range(DC):
                    if c == DC // 2:
                        ahead(n)
                    act.wait_ge(h_ready, fill * DC + c + 1)
                    moving_hi(m_hi, H, c)

            def square(b, full):
                act.wait_ge(*full)
                nc.scalar.activation(sq[:, 2 * b:2 * b + 2, :], X[b][:], ACT.Square).then_inc(sq_ready, 1)

            def root(k):
                u = use[f"norm{k}"]
                nc.scalar.activation(warm[:, k:k + 1], ones[:, 0:1], ACT.Sqrt)
                act.wait_ge(bank_full, u + 1)
                nc.scalar.activation(rstd[:], bank[u % BANKS][:, 0:T], ACT.Sqrt, bias=eps[:], scale=1.0 / D)\
                  .then_inc(bank_read[u % BANKS], 1)

            def rope_copy(k, dst, n):
                act.wait_ge(bank_full, k + 1)
                if n >= 2:
                    act.wait_ge(rope_out, n - 1)
                b = bank[k % BANKS]
                nc.scalar.activation(dst, cols(b), ACT.Copy)
                nc.scalar.activation(swap[0:64, n % 2, :], b[64:128, 0:T], ACT.Copy)
                nc.scalar.activation(swap[64:128, n % 2, :], b[0:64, 0:T], ACT.Copy)\
                  .then_inc(bank_read[k % BANKS], 1)

            def exps(l, i):
                h = attention_heads(l)[i]
                act.wait_ge(max_ready, MEM_HEADS * l + i + 1)
                for t in range(TT):
                    e = nc.scalar.activation(probs[h][:, t, :], probs[h][:, t, :], ACT.Exp,
                                             bias=nmax[:, h, t:t + 1], accum_out=rsum[:, h, t:t + 1])
                e.then_inc(exp_ready, 1)

            def attention(l):
                heads = attention_heads(l)
                base = MEM_HEADS if l == 1 else 0

                def pt(i):
                    k = use[l, "pt", heads[i]]
                    copy_out(k, pT[(base + i) % 2], lambda b: b[:].rearrange("p (c t) -> p c t", c=2))

                if l == 0:
                    for n in range(DC):
                        ahead(slot[0, "pool"] + n * 2 // DC)
                        upper_out(use[0, "pool", 0] + n, mix_hi[:, n, :], G[:, 6, n:n + 1])
                    for i in range(2, MEM_HEADS):
                        exps(0, i)

                def mixed(i):
                    k = use[l, "pv", heads[i]]
                    act.wait_ge(bank_full, k + 1)
                    nc.scalar.activation(mix_hi[:, heads[i], :], cols(bank[k % BANKS]), ACT.Copy)
                    copy_out(k, probs[heads[i]][:, 0, :], cols)

                for i in range(len(heads)):
                    pt(i)
                    if i:
                        mixed(i - 1)
                    if l and i + 3 < len(heads):
                        exps(1, i + 3)
                mixed(len(heads) - 1)

            def memory_key(l, n, k):
                ahead(slot[l, "memk"] + n)
                copy_out(k, memKT[:, n, :], cols)

            def memory_values(l):
                for n in range(MEM_HEADS):
                    ahead(slot[l, "memv"] + n)
                    copy_out(use[l, "memv"] + n, memVT[:, n, :], cols)
                    for c in (2 * n, 2 * n + 1) if l == 0 else ():
                        act.wait_ge(window_ready, n + 1)
                        moving_hi(m_hi, (win_a, win_b)[n % 2], c)
                    if l == 0 and n < 2:
                        exps(0, n)

            def values_over_tokens(l):
                for c in range(2):
                    copy_out(use[l, "memvt"] + c, memV[:, c, :], lambda b: b[:])

            for l in range(2):
                if l == 0:
                    act.dma_start(memT, mem_in).then_inc(mem_loaded, 16)
                    act.dma_start(inv_count, tables[:, 4:8, :]).then_inc(table_loaded, 16)
                    ahead(-LEAD)
                    act.wait_ge(mem_loaded, 16)
                    for c in range(DC):
                        moving_hi(mem_hi, memT, c)
                    ahead(2 - LEAD)
                    for b in range(DC // 2):
                        square(b, (x_full, b + 1))
                    for n in range(2):
                        memory_key(0, n, use[0, "memk"] + n)
                    act.wait_ge(eps_ready, 1)
                    act.wait_ge(const_loaded, 16)
                    root(0)
                    ahead(slot[0, "memk"] + MEM_HEADS - 1)
                    h_hi(0, slot[0, "in"])
                    for n in range(2, MEM_HEADS):
                        memory_key(0, n, use[0, "memk2"] + n - 2)
                k = use[l, "in"]
                for n in range(DC):
                    ahead(slot[l, "in"] + n)
                    if l == 0:
                        copy_out(k + n, mainT[:, n, :], cols)
                    else:
                        rope_copy(k + n, qT[:, n, :], MOBA_HEADS + n)
                for n in range(MEM_HEADS):
                    ahead(slot[l, "in"] + DC + n)
                    copy_out(use[l, "qm", n], qmT[:, n, :], cols)
                    if l and n:
                        exps(1, n - 1)
                if l == 0:
                    memory_values(0)
                    values_over_tokens(0)
                attention(l)
                for i in range(MIXC):
                    ahead(slot[l, "out"] + i)
                    if i % 3 == 2:
                        b = i // 3
                        square(b, (x_full, DC // 2 * (l + 1) + b + 1))
                root(1 if l == 0 else 3)
                h_hi(1 if l == 0 else 4, slot[l, "wq"])
                k = use[l, "wq"]
                for n in range(PAIRS):
                    ahead(slot[l, "wq"] + n)
                    upper_out(k + n, qp_hi[:, n, :])
                k = use[l, "score"]
                for n in range(PAIRS):
                    ahead(slot[l, "keys"] + n // DC)
                    act.wait_ge(bank_full, k + n + 1)
                    nc.scalar.activation(score[:, :, n, :], scores_of(bank[(k + n) % BANKS])[:, :, 1, :], ACT.Copy)\
                      .then_inc(score_part, 1)
                assert hi_done[0] == slot[l, "keys"] + 1 + LEAD + 1
                u, v = slot[l, "u"], slot[l, "v"]
                def gelu(i, e, b, read):
                    nc.scalar.activation(A[:, bass.ds(i * BODY + e, 1), :],
                                         bank[b][:, 0:T].rearrange("p (a b) -> p a b", a=1), ACT.Gelu).then_inc(read, 1)

                def early_gelu(i, e):
                    weight_hi(i, u + e + LEAD)
                    k = use[l, "up0"] + e
                    act.wait_ge(bank_full, i * BODY + (k + 1))
                    gelu(i, e, k % BANKS, bank_read[k % BANKS])

                def late_gelu(i, a):
                    e = KEYS - LATE + a
                    weight_hi(i, u + e + LEAD)
                    act.wait_ge(act_full, i * BODY + (LATE * l + a + 1))
                    gelu(i, e, a % 2, act_read)

                with act.Fori(0, TURNS - 1) as i:
                    for j in range(BODY):
                        early_gelu(i, j)
                act.wait_ge(cdiff_ready, l + 1)
                nc.scalar.activation(cexp, gate, ACT.Exp).then_inc(cexp_ready, 1)
                for j in range(BODY // 2):
                    early_gelu(0, HALF - BODY + j)
                for n, dst in enumerate((e1T, e2T, gT)):
                    copy_out(use[l, "routeT"] + n, dst[:], cols, GATE_SCALE if dst is gT else 1.0)
                for a in range(BODY // 2):
                    late_gelu(0, a)
                with act.Fori(0, TURNS) as i:
                    for j in range(BODY):
                        late_gelu(i, BODY // 2 + j)
                for half in range(2):
                    act.wait_ge(gate_read, GBLK * (2 * l + half + 1) + l + 1)
                    for j in range(MLEAD):
                        tile_hi(0, half, j)

                    def turn(i, last):
                        for j in range(BODY):
                            n = v + half * HALF + j + LEAD
                            if n + (i * BODY if last else 0) < n_slots:
                                weight_hi(i, n)
                            if not (last and j + MLEAD >= BODY):
                                tile_hi(i, half, j + MLEAD)
                            elif half == 1 and l == 0:
                                if j == BODY - MLEAD:
                                    act.wait_ge(mem_loaded, 32)
                                for c in range(DC // MLEAD):
                                    moving_hi(mem_hi, memT, (j + MLEAD - BODY) * (DC // MLEAD) + c)

                    with act.Fori(0, TURNS - 1) as i:
                        turn(i, False)
                    if half == 1 and l == 0:
                        act.wait_ge(mov_lo, part[l, "tile"] + KEYS - BODY)
                        act.dma_start(memT, mem_in).then_inc(mem_loaded, 16)
                        act.dma_start(at(36, 4), tables[:, 0:4, :]).then_inc(table_loaded, 16)
                    turn(TURNS - 1, True)
                hi_done[0] = min(v + KEYS + LEAD, n_slots)
                for b in range(DC // 2):
                    square(b, (down_done, KEYS * (l + 1)))
                if l == 0:
                    memory_key(1, 0, use[1, "memk"])
                    root(2)
                    ahead(slot[1, "memk"] + 1)
                    h_hi(2, slot[1, "memk"] + 2)
                    for n in range(1, MEM_HEADS):
                        memory_key(1, n, use[1, "memk2"] + n - 1)
                    memory_values(1)
                    k = use["kv"]
                    for n in range(MOBA_HEADS):
                        ahead(slot[1, "kv"] + n)
                        rope_copy(k + n, keyT[:, n, :], n)
                    for n in range(MOBA_HEADS):
                        ahead(slot[1, "kv"] + 8 + n)
                        copy_out(k + 8 + n, valT[:, n, :], cols)
                    values_over_tokens(1)
                    for c in range(2):
                        for q in range(2):
                            copy_out(use["kvt"] + 2 * c + q, val[:, c, q * 512:(q + 1) * 512], lambda b: b[:])
                    h_hi(3, slot[1, "in"])
            root(4)

        @block.vector
        def _(dve):
            steps = [0]

            def after(ins):
                steps[0] += 1
                ins.then_inc(dve_step, 1)
                dve.wait_ge(dve_step, steps[0])

            def copied(k):
                dve.wait_ge(bank_read[k % BANKS], k // BANKS + 1)

            products = [0]

            def product_lo(k, hi, lo, scale=None):
                products[0] += 1
                dve.wait_ge(out_hi, products[0])
                src = bank[k % BANKS][:, 0:T]
                if scale is None:
                    ins = nc.vector.tensor_tensor(lo, src, hi.bitcast(F32), ALU.subtract)
                else:
                    ins = nc.vector.scalar_tensor_tensor(lo, src, scale, hi.bitcast(F32), ALU.mult, ALU.subtract)
                ins.then_inc(bank_read[k % BANKS], 1)

            def parts_lo(name, src, dst_lo=None, dst_hi=None):
                for c in range(DC):
                    part_lo((dst_lo or m_lo)[:, c, :], src(c), (dst_hi or m_hi)[:, c, :].bitcast(F32), part[name] + c + 1)

            def part_lo(dst, src, hi, n):
                dve.wait_ge(mov_hi, n)
                nc.vector.tensor_tensor(dst, src, hi, ALU.subtract).then_inc(mov_lo, 1)

            def norm_scale(k):
                copied(use[f"norm{k}"])
                after(nc.vector.reciprocal(rstd[:], rstd[:]))

            def norm_fill(gain):
                for c in range(DC):
                    fill(gain, c)

            def fill(gain, c):
                nc.vector.scalar_tensor_tensor(H[:, c, :], X[c // 2][:, c % 2, :], G[:, gain, c:c + 1], rstd[:],
                                               ALU.mult, ALU.mult).then_inc(h_ready, 1)

            def norm_fill_and_lo(gain, name):
                for c in range(DC + 1):
                    if c < DC:
                        fill(gain, c)
                    if c:
                        part_lo(m_lo[:, c - 1, :], H[:, c - 1, :], m_hi[:, c - 1, :].bitcast(F32), part[name] + c)

            def rope(buf, n, k):
                copied(k)
                a, b = buf, swap[:, n % 2, :]
                nc.vector.tensor_tensor(a, a, cos, ALU.mult)
                after(nc.vector.tensor_tensor(b, b, sin, ALU.mult))
                nc.vector.tensor_tensor(a, a, b, ALU.add).then_inc(rope_out, 1)

            def windows():
                dve.wait_ge(table_loaded, 16)
                for g, w in enumerate(WINDOWS):
                    a, b = 2 * g, 2 * g + 2
                    copied(use[0, "in"] + b - 1)
                    src, dst, other = mainT, win_a, win_b
                    for i in range(g + 1):
                        n = 2 ** i
                        nc.vector.tensor_tensor(dst[:, a:b, n:T], src[:, a:b, n:T], src[:, a:b, 0:T - n], ALU.add)
                        after(nc.vector.tensor_copy(dst[:, a:b, 0:n], src[:, a:b, 0:n]))
                        src, dst, other = dst, other, dst
                    assert w == 2 * n
                    r = src[:, a:b, :]
                    after(nc.vector.tensor_tensor(r, r, inv_count[:, g:g + 1, :].broadcast_to([P, 2, T]), ALU.mult))
                    nc.vector.tensor_tensor(r, r, mainT[:, a:b, :], ALU.subtract).then_inc(window_ready, 1)

            def attention(l):
                heads = attention_heads(l)
                base = MEM_HEADS if l == 1 else 0

                def maxima(i):
                    h = heads[i]
                    k = use[l, "qk", h]
                    dve.wait_ge(bank_full, k + 1)
                    p = probs[h]
                    src = bank[k % BANKS][:].rearrange("p (t k) -> p t k", t=TT)
                    if h < MOBA_HEADS:
                        ins = nc.vector.scalar_tensor_tensor(p, src, SCALE, mask, ALU.mult, ALU.add)
                    else:
                        ins = nc.vector.tensor_scalar(p, src, SCALE, None, ALU.mult)
                    ins.then_inc(bank_read[k % BANKS], 1)
                    copied(k)
                    after(nc.vector.tensor_reduce(rinv[:, h, :], p, AX, ALU.max))
                    nc.vector.tensor_scalar(nmax[:, h, :], rinv[:, h, :], -1.0, None, ALU.mult).then_inc(max_ready, 1)

                def scale(i):
                    h = heads[i]
                    dve.wait_ge(exp_ready, base + i + 1)
                    after(nc.vector.reciprocal(rinv[:, h, :], rsum[:, h, :]))
                    for t in range(TT):
                        ins = nc.vector.tensor_scalar(probs[h][:, t, :], probs[h][:, t, :], rinv[:, h, t:t + 1], None, ALU.mult)
                    ins.then_inc(prob_ready, 1)

                def lower_out(i):
                    h = heads[i]
                    copied(use[l, "pv", h])
                    nc.vector.tensor_tensor(mix_lo[:, h, :], probs[h][:, 0, :], mix_hi[:, h, :].bitcast(F32),
                                            ALU.subtract).then_inc(head_lo, 1)

                if l == 0:
                    for i in range(MEM_HEADS):
                        maxima(i)
                    for i in range(MEM_HEADS):
                        for c in (2 * i, 2 * i + 1):
                            part_lo(m_lo[:, c, :], (win_a, win_b)[i % 2][:, c, :], m_hi[:, c, :].bitcast(F32),
                                    part[0, "window"] + c + 1)
                    for i in range(2):
                        scale(i)
                    for n in range(DC):
                        product_lo(use[0, "pool", 0] + n, mix_hi[:, n, :], mix_lo[:, n, :], G[:, 6, n:n + 1])
                    for i in range(2, MEM_HEADS):
                        scale(i)
                    for i in range(MEM_HEADS):
                        lower_out(i)
                    return
                for i in range(3):
                    maxima(i)
                for i in range(len(heads)):
                    scale(i)
                    if i + 3 < len(heads):
                        maxima(i + 3)
                    if i > 1:
                        lower_out(i - 2)
                lower_out(len(heads) - 2)
                lower_out(len(heads) - 1)

            def top16(values, spare, best, where):
                n = len(values)
                for i in range(n):
                    ins = nc.vector.max(best[i][:, 0:8], values[i])
                after(ins)
                for i in range(n):
                    nc.vector.max_index(where[i][:, 0:8], best[i][:, 0:8], values[i])
                    ins = nc.vector.match_replace(spare[i], best[i][:, 0:8], values[i], TAKEN)
                after(ins)
                for i in range(n):
                    ins = nc.vector.max(best[i][:, 8:16], spare[i])
                after(ins)
                for i in range(n):
                    ins = nc.vector.max_index(where[i][:, 8:16], best[i][:, 8:16], spare[i])
                after(ins)

            def choose(l):
                for n in range(PAIRS):
                    k = use[l, "score"] + n
                    dve.wait_ge(score_part, PAIRS * l + n + 1)
                    nc.vector.tensor_tensor(score[:, :, n, :], scores_of(bank[k % BANKS])[:, :, 0, :], score[:, :, n, :], ALU.add)\
                      .then_inc(bank_read[k % BANKS], 1)
                copied(use[l, "score"] + PAIRS - 1)
                ts = [(t, s) for t in range(TT) for s in range(PAIRS)]
                top16([score[:, t, s, :] for t, s in ts], [rest[:, t, s, :] for t, s in ts],
                      [sv[:, t, s, :] for t, s in ts], [si[:, t, s, :] for t, s in ts])
                nc.vector.tensor_copy(sif, si.rearrange("p t s k -> p (t s k)"))
                v = sv.rearrange("p t (h s) k -> p (t h) s k", s=2)
                R = TT * PH
                c4 = cand.rearrange("p (r i j) -> p r i j", r=R, i=TOPK)
                shape = [P, R, TOPK, TOPK]
                after(nc.vector.tensor_tensor(c4, v[:, :, 0, :, None].broadcast_to(shape),
                                              v[:, :, 1, None, :].broadcast_to(shape), ALU.add))
                C = TOPK * TOPK
                top16([cand[:, r * C:(r + 1) * C] for r in range(R)], [cand_rest[:, r * C:(r + 1) * C] for r in range(R)],
                      [cv[:, r * TOPK:(r + 1) * TOPK] for r in range(R)], [ci[:, r * TOPK:(r + 1) * TOPK] for r in range(R)])
                c3 = cv.rearrange("p (r k) -> p r k", r=R)
                g3v = gate.rearrange("p (r k) -> p r k", r=R)
                nc.vector.tensor_tensor(g3v, c3, c3[:, :, 0:1].broadcast_to([P, R, TOPK]), ALU.subtract).then_inc(cdiff_ready, 1)
                nc.vector.tensor_scalar(pos1, ci, 4, None, ALU.logical_shift_right)
                after(nc.vector.tensor_scalar(pos2, ci, TOPK - 1, None, ALU.bitwise_and))
                nc.vector.tensor_copy(pos1f, pos1)
                after(nc.vector.tensor_copy(pos2f, pos2))
                sf = sif.rearrange("p (r s k) -> p r s k", r=R, s=2)
                for side, (pos, hit, e) in enumerate(((pos1f, hit1, e1), (pos2f, hit2, e2))):
                    h3 = hit.rearrange("p (a j) -> p a j", j=TOPK)
                    after(nc.vector.tensor_tensor(h3, pos[:, :, None].broadcast_to([P, R * TOPK, TOPK]),
                                                  iota[:, None, 0:TOPK].broadcast_to([P, R * TOPK, TOPK]), ALU.is_equal))
                    h4 = hit.rearrange("p (r k j) -> p r k j", r=R, k=TOPK)
                    after(nc.vector.tensor_tensor(h4, h4, sf[:, :, side, None, :].broadcast_to(shape), ALU.mult))
                    after(nc.vector.tensor_reduce(e, h3, AX, ALU.add))
                dve.wait_ge(cexp_ready, l + 1)
                x3 = cexp.rearrange("p (r k) -> p r k", r=R)
                after(nc.vector.tensor_reduce(csum, x3, AX, ALU.add))
                after(nc.vector.reciprocal(cinv, csum))
                nc.vector.tensor_tensor(g3v, x3, cinv[:, :, None].broadcast_to([P, R, TOPK]), ALU.mult).then_inc(route_ready, 1)

            def split_gates(l):
                copied(use[l, "routeT"] + 2)
                after(nc.vector.tensor_copy(g2[:, :, 0], gT[:]))
                nc.vector.tensor_copy(iota_bank, iota)
                nc.vector.tensor_copy(g_first, g2[:, :, 0]).then_inc(gate_read, 1)
                after(nc.vector.tensor_tensor(g2[:, :, 1], gT[:], g2[:, :, 0], ALU.subtract))

            def one(a):
                return a.rearrange("p (a b) -> p a b", a=1)

            def gates_and_tiles(l, gate_half, tile_half):
                half = gate_half
                first = None if half is None else GBLK * (2 * l + half)

                def build(half, i, b, begin=False):
                    ts = bass.ds(i * (TOK * BODY) + b % GBLK * TOK, TOK)
                    buf = b % 2
                    if not begin or l:
                        dve.wait_ge(hot_ready, i * BODY + (first + b))
                    nc.vector.tensor_tensor(hot1[:, buf], iota_bank[:, None, :].broadcast_to([P, TOK, P]),
                                            e1T[:, ts, None].broadcast_to([P, TOK, P]), ALU.is_equal)
                    nc.vector.tensor_tensor(hot2[:], iota_bank[:, None, half * HALF:(half + 1) * HALF].broadcast_to([P, TOK, HALF]),
                                            e2T[:, ts, None].broadcast_to([P, TOK, HALF]), ALU.is_equal).then_inc(dve_step, 1)
                    dve.wait_ge(dve_step, i * BODY + (steps[0] + b + 1))
                    for p, g in enumerate((g_first[:, ts, None], g2[:, ts, 1, None])):
                        ins = nc.vector.tensor_tensor(hotg[:, buf, :, p, :], hot2[:], g.broadcast_to([P, TOK, HALF]), ALU.mult)
                    ins.then_inc(hot_ready, 1)

                def apply(i, b):
                    dve.wait_ge(gate_full, i * BODY + (first + b + 1))
                    a = A[:, half * HALF:(half + 1) * HALF, bass.ds(i * (TOK * BODY) + b * TOK, TOK)].rearrange("p e t -> p t e")
                    nc.vector.scalar_tensor_tensor(a, bank[GATE_BANK][:, 0:TOK * HALF].rearrange("p (t e) -> p t e", t=TOK),
                                                   1.0 / GATE_SCALE, a, ALU.mult, ALU.mult)\
                      .then_inc(gate_read, 1)

                def tile_lo(i, j):
                    e = tile_half * HALF + j
                    part_lo(one(m_lo[:, j % BODY, :]), A[:, bass.ds(i * BODY + e, 1), :], one(m_hi[:, j % BODY, :].bitcast(F32)),
                            i * BODY + (part[l, "tile"] + e + 1))

                def turn(i, last):
                    for j in range(BODY):
                        if half is not None:
                            if not (last and j + 1 >= BODY):
                                build(half, i, j + 1)
                            elif half == 0:
                                build(1, 0, GBLK)
                            apply(i, j)
                        if tile_half is not None and not (last and j + MLEAD >= BODY):
                            tile_lo(i, j + MLEAD)

                if tile_half is not None:
                    for j in range(MLEAD):
                        tile_lo(0, j)
                if half is not None:
                    dve.wait_ge(act_read, LATE * (l + half) + (BODY // 2 if half == 0 else 0))
                    if half == 0:
                        build(0, 0, 0, begin=True)
                with dve.Fori(0, TURNS - 1) as i:
                    turn(i, False)
                turn(TURNS - 1, True)
                if half is not None:
                    steps[0] += GBLK

            nc.vector.memset(eps[:], EPS).then_inc(eps_ready, 1)
            for l in range(2):
                if l == 0:
                    parts_lo((0, "mem"), lambda c: memT[:, c, :], mem_lo, mem_hi)
                    dve.wait_ge(const_loaded, 16)
                    dve.wait_ge(gains_loaded, 16)
                    norm_scale(0)
                    norm_fill_and_lo(0, (0, "h_mix"))
                    windows()
                else:
                    parts_lo((1, "h_mix"), lambda c: H[:, c, :])
                    for n in range(MOBA_HEADS):
                        rope(qT[:, n, :], MOBA_HEADS + n, use[l, "in"] + n)
                attention(l)
                norm_scale(1 if l == 0 else 3)
                norm_fill_and_lo(3 if l == 0 else 4, (l, "h_ffn"))
                for n in range(PAIRS):
                    product_lo(use[l, "wq"] + n, qp_hi[:, n, :], qp_lo[:, n, :])
                choose(l)
                split_gates(l)
                gates_and_tiles(l, 0, None)
                gates_and_tiles(l, 1, 0)
                gates_and_tiles(l, None, 1)
                if l == 0:
                    parts_lo((1, "mem"), lambda c: memT[:, c, :], mem_lo, mem_hi)
                    norm_scale(2)
                    norm_fill_and_lo(2, "h_kv")
                    dve.wait_ge(mov_lo, part["h_kv"] + DC)
                    norm_fill(1)
                    dve.wait_ge(table_loaded, 32)
                    for n in range(MOBA_HEADS):
                        rope(keyT[:, n, :], n, use["kv"] + n)
            norm_scale(4)
            norm_fill(5)


def kernel(x, mem, norm_mix_g, w_in, w_out, w_mem_kv, pool_w, pool_scale, kv_norm_g, w_kv_shared,
           norm_ffn_g, peer_wq, peer_subkeys, peer_u, peer_v, final_norm_g):
    import numpy as np
    import concourse.bacc as bacc
    from concourse.bass_utils import run_bass_kernel_spmd

    def arr(a):
        return np.asarray(a)

    def blocks(w):
        k, n = w.shape
        return w.reshape(k // P, P, n // P, P).transpose(2, 0, 1, 3).reshape(-1, P, P)

    def pack(tiles):
        return tiles.reshape(-1, DC, P, P).transpose(0, 2, 1, 3).reshape(-1, P, D)

    def columns(v):
        return arr(v).reshape(DC, P).T

    def chunks(a):
        return np.ascontiguousarray(arr(a).reshape(-1, DC, P).transpose(2, 1, 0))

    _, slot, _, n_slots = plan()
    stream = np.empty((n_slots, P, D), np.float32)
    for l, names in enumerate(LAYER_SLOTS):
        for name in names:
            s = slot[l, name]
            place = stream[s:s + SLOTS[name]]
            if name in ("memk", "memv"):
                a = MEM_HEADS * HD * (name == "memv")
                place[:] = pack(blocks(arr(w_mem_kv)[l][:, a:a + MEM_HEADS * HD]))
            elif name == "in":
                place[:] = pack(blocks(arr(w_in)[l]))
            elif name == "pool":
                place[:] = pack(np.concatenate([blocks(w) for w in arr(pool_w)[l]]))
            elif name == "out":
                place[:] = pack(blocks(arr(w_out)[l]))
            elif name == "wq":
                place[:] = pack(blocks(arr(peer_wq)[l]))
            elif name == "keys":
                place[:] = pack(arr(peer_subkeys)[l].reshape(PAIRS, KEYS, P).transpose(0, 2, 1))
            elif name == "kv":
                place[:] = pack(blocks(arr(w_kv_shared)))
            elif name == "u":
                u = arr(peer_u)[l].reshape(KEYS, KEYS, DC, P)
                place[:] = u.transpose(1, 3, 2, 0).reshape(KEYS, P, D)
            else:
                place[:] = arr(peer_v)[l].reshape(KEYS, KEYS, D).transpose(1, 0, 2)
    gains = np.stack([columns(g) for g in (arr(norm_mix_g)[0], arr(norm_mix_g)[1], kv_norm_g, arr(norm_ffn_g)[0],
                                           arr(norm_ffn_g)[1], final_norm_g, arr(pool_scale)[0])], axis=1)
    small = np.stack([np.eye(P), np.tile(np.arange(P), (P, 1)), np.ones((P, P))], axis=1).astype(np.float32)
    t = np.arange(T)
    inv = np.float32(1.0) / (np.float32(10000.0) ** (np.arange(0, HD, 2, dtype=np.float32) / np.float32(HD)))
    angle = (t.astype(np.float32)[:, None] * inv[None, :]).T
    cos, sin = np.cos(angle), np.sin(angle)
    tables = np.zeros((P, 8, T), np.float32)
    tables[:, 0] = np.concatenate([cos, cos])
    tables[:, 1] = np.concatenate([-sin, sin])
    for i in range(TT):
        tables[:, 2 + i] = np.where(t[None, :] <= (i * P + np.arange(P))[:, None], 0.0, NEG)
    for g, w in enumerate(WINDOWS):
        tables[:, 4 + g] = 1.0 / np.minimum(t + 1, w)

    arrays = {"stream": stream.reshape(n_slots * P, D), "x_in": chunks(arr(x)[0]), "mem_in": chunks(arr(mem)[0]),
              "gains": np.ascontiguousarray(gains), "small": small, "tables": tables}
    nc = bacc.Bacc("TRN2", target_bir_lowering=False, num_devices=1)
    args = [nc.dram_tensor(n, a.shape, mybir.dt.from_np(a.dtype), kind="ExternalInput").ap() for n, a in arrays.items()]
    out = nc.dram_tensor("out", (P, DC, T), F32, kind="ExternalOutput").ap()
    build(nc, *args, out)
    r = run_bass_kernel_spmd(nc, [arrays], core_ids=[0])
    return r.results[0]["out"].transpose(2, 1, 0).reshape(1, T, D)
```
